# Optimizing a Trainium2 kernel written in Bass

```python
import math
import jax, jax.numpy as jnp
from jax import lax
import numpy as np

D_MODEL = 1024
BATCH = 1
SEQ = 512
DEPTH = 1

GRID_W = 64
CTX_LEN = 256

F_GROUPS = 4
F_GROUP_DIM = 128
F_WIDTH = F_GROUPS * F_GROUP_DIM

DN_HEADS = 8
DN_HEAD_DIM = 128
DN_WIDTH = DN_HEADS * DN_HEAD_DIM
DN_CHUNK = 64
SHORT_CONV = 5
N_DIR = 2

N_BRANCH = 2

COL_A = 0
COL_B = COL_A + N_DIR * DN_HEADS
COL_K = COL_B + N_DIR * DN_HEADS
COL_V = COL_K + DN_WIDTH
COL_Q = COL_V + DN_WIDTH
COL_Z = COL_Q + DN_WIDTH
COL_F = COL_Z + DN_WIDTH
COL_G = COL_F + F_WIDTH
IN_COLS = COL_G + N_BRANCH * D_MODEL

PEER_HEADS = 8
PEER_N_KEYS = 128
PEER_EXPERTS = PEER_N_KEYS * PEER_N_KEYS
PEER_KEY_DIM = 256
PEER_TOPK = 16
PEER_TOKEN_BLOCK = 128

N_MOD = 6

DEEPNORM_ALPHA = (2 * DEPTH) ** 0.25
DEEPNORM_BETA = (8 * DEPTH) ** -0.25
LN_EPS = 1e-6
RMS_EPS = 1e-6
L2_EPS = 1e-6

kernel_name = "hybrid_fnet_deltanet_peer_dit_layer"

def layer_norm(x):
    xf = x.astype(jnp.float32)
    mu = jnp.mean(xf, axis=-1, keepdims=True)
    var = jnp.mean(jnp.square(xf - mu), axis=-1, keepdims=True)
    return ((xf - mu) * lax.rsqrt(var + LN_EPS)).astype(x.dtype)

def post_norm(resid, update, gain, bias):
    return layer_norm(DEEPNORM_ALPHA * resid + update) * gain + bias

def modulate(h, shift, scale):
    return h * (1.0 + scale) + shift

def ada_modulation(cond, w, b, n):
    m = jax.nn.silu(cond) @ w[:, :n * D_MODEL] + b[:n * D_MODEL]
    return m.reshape(m.shape[:-1] + (n, D_MODEL))

def l2norm(t):
    return t * lax.rsqrt(jnp.sum(jnp.square(t), axis=-1, keepdims=True) + L2_EPS)

def heads(t):
    return t.reshape(t.shape[:2] + (DN_HEADS, DN_HEAD_DIM))

def short_conv(t, w):
    pad = SHORT_CONV // 2
    return lax.conv_general_dilated(
        t, w[:, None, :].astype(t.dtype), window_strides=(1,), padding=[(pad, pad)],
        dimension_numbers=('NWC', 'WIO', 'NWC'), feature_group_count=t.shape[-1])

def latent_conv(t, w):
    b, s, ch = t.shape
    rows = s // GRID_W
    return short_conv(t.reshape(b * rows, GRID_W, ch), w).reshape(b, s, ch)

def fourier_mix(f):
    b, l, _ = f.shape
    fg = f.astype(jnp.float32).reshape(b, l, F_GROUPS, F_GROUP_DIM)
    y = jnp.real(jnp.fft.fft2(fg, axes=(1, 3), norm='ortho'))
    return y.reshape(b, l, F_WIDTH).astype(f.dtype)

def _to_chunks(t):
    b, l, h = t.shape[:3]
    t = t.reshape((b, l // DN_CHUNK, DN_CHUNK, h) + t.shape[3:])
    return jnp.transpose(t, (1, 0, 3, 2) + tuple(range(4, t.ndim)))

def _delta_state_step(s, u_i, w_i, kd_i, gl_i):
    v_new = u_i - jnp.einsum('bhck,bhkv->bhcv', w_i, s)
    s_next = s * jnp.exp(gl_i)[..., None, None] + jnp.einsum('bhck,bhcv->bhkv', kd_i, v_new)
    return v_new, s_next

def gated_delta_chunked(k, v, g, beta, s0, q):
    b, l, h, _ = k.shape
    dv = v.shape[-1]
    kc, vc, bc = _to_chunks(k), _to_chunks(v), _to_chunks(beta)
    gc = jnp.cumsum(_to_chunks(g), axis=-1)
    idx = jnp.arange(DN_CHUNK)
    incl = idx[:, None] >= idx[None, :]
    strict = idx[:, None] > idx[None, :]
    decay = jnp.exp(jnp.where(incl, gc[..., :, None] - gc[..., None, :], -jnp.inf))
    kb = kc * bc[..., None]
    lmat = jnp.where(strict, jnp.einsum('nbhid,nbhjd->nbhij', kb, kc) * decay, 0.0)
    amat = lmat + jnp.eye(DN_CHUNK, dtype=lmat.dtype)
    rhs = jnp.concatenate([vc * bc[..., None], kb * jnp.exp(gc)[..., None]], axis=-1)
    sol = lax.linalg.triangular_solve(amat, rhs, left_side=True, lower=True, unit_diagonal=True)
    u, w = sol[..., :dv], sol[..., dv:]
    g_last = gc[..., -1]
    k_dec = kc * jnp.exp(g_last[..., None] - gc)[..., None]
    if q is None:
        def step_state(s, xs):
            _, s_next = _delta_state_step(s, *xs)
            return s_next, None
        s_fin, _ = lax.scan(step_state, s0, (u, w, k_dec, g_last))
        return None, s_fin
    qc = _to_chunks(q)
    q_dec = qc * jnp.exp(gc)[..., None]
    attn = jnp.where(incl, jnp.einsum('nbhid,nbhjd->nbhij', qc, kc) * decay, 0.0)

    def step(s, xs):
        u_i, w_i, kd_i, gl_i, qd_i, a_i = xs
        v_new, s_next = _delta_state_step(s, u_i, w_i, kd_i, gl_i)
        o_i = jnp.einsum('bhck,bhkv->bhcv', qd_i, s) + jnp.einsum('bhij,bhjv->bhiv', a_i, v_new)
        return s_next, o_i
    s_fin, o = lax.scan(step, s0, (u, w, k_dec, g_last, q_dec, attn))
    o = jnp.transpose(o, (1, 0, 3, 2, 4)).reshape(b, l, h, dv)
    return o, s_fin

def delta_inputs(p, kvq, a_log, dt_bias, with_q):
    kvq = kvq.astype(jnp.float32)
    p = p.astype(jnp.float32)
    k = l2norm(heads(kvq[..., :DN_WIDTH]))
    v = heads(kvq[..., DN_WIDTH:2 * DN_WIDTH])
    q = l2norm(heads(kvq[..., 2 * DN_WIDTH:3 * DN_WIDTH])) * (DN_HEAD_DIM ** -0.5) if with_q else None
    dir_shape = p.shape[:2] + (N_DIR, DN_HEADS)
    a_in = p[..., COL_A:COL_B].reshape(dir_shape)
    b_in = p[..., COL_B:COL_K].reshape(dir_shape)
    g = -jnp.exp(a_log.astype(jnp.float32)) * jax.nn.softplus(a_in + dt_bias.astype(jnp.float32))
    beta = jax.nn.sigmoid(b_in)
    return q, k, v, g, beta

def _orient(t, d):
    return t if (t is None or d == 0) else jnp.flip(t, axis=1)

def bidir_delta(lat, ctx_in):
    qx, kx, vx, gx, bx = lat
    qc, kc, vc, gc, bc = ctx_in
    s0 = jnp.zeros((kx.shape[0], DN_HEADS, DN_HEAD_DIM, DN_HEAD_DIM), jnp.float32)

    def one_direction(d):
        o_c, s_c = gated_delta_chunked(_orient(kc, d), _orient(vc, d), _orient(gc[:, :, d], d),
                                       _orient(bc[:, :, d], d), s0, _orient(qc, d))
        o_x, _ = gated_delta_chunked(_orient(kx, d), _orient(vx, d), _orient(gx[:, :, d], d),
                                     _orient(bx[:, :, d], d), s_c, _orient(qx, d))
        return _orient(o_x, d), _orient(o_c, d)

    ox_f, oc_f = one_direction(0)
    ox_b, oc_b = one_direction(1)
    o_ctx = None if qc is None else oc_f + oc_b
    return ox_f + ox_b, o_ctx

def gated_rmsnorm(o, z, w):
    y = o * lax.rsqrt(jnp.mean(jnp.square(o), axis=-1, keepdims=True) + RMS_EPS) * w.astype(jnp.float32)
    return (y * jax.nn.silu(z.astype(jnp.float32))).astype(z.dtype)

def merge_branches(p, o_dn, dn_norm_w, w_four, w_dn, w_out):
    b, l, _ = p.shape
    four = fourier_mix(p[..., COL_F:COL_G]) @ w_four
    dn = gated_rmsnorm(o_dn, heads(p[..., COL_Z:COL_F]), dn_norm_w).reshape(b, l, DN_WIDTH) @ w_dn
    gates = jax.nn.sigmoid(p[..., COL_G:].reshape(b, l, N_BRANCH, D_MODEL))
    return (gates[:, :, 0] * four + gates[:, :, 1] * dn) @ w_out

def token_mixer(hx, hc, w_in, conv_w, a_log, dt_bias, dn_norm_w, w_four, w_dn, w_out, ctx_out):
    px = hx @ w_in
    pc = hc @ w_in[:, :(IN_COLS if ctx_out else COL_Q)]
    kvq_x = jax.nn.silu(latent_conv(px[..., COL_K:COL_Z], conv_w))
    n_ctx_conv = (COL_Z if ctx_out else COL_Q) - COL_K
    kvq_c = jax.nn.silu(short_conv(pc[..., COL_K:COL_K + n_ctx_conv], conv_w[:, :n_ctx_conv]))
    lat = delta_inputs(px, kvq_x, a_log, dt_bias, True)
    ctx_in = delta_inputs(pc, kvq_c, a_log, dt_bias, ctx_out)
    o_x, o_c = bidir_delta(lat, ctx_in)
    y_x = merge_branches(px, o_x, dn_norm_w, w_four, w_dn, w_out)
    y_c = merge_branches(pc, o_c, dn_norm_w, w_four, w_dn, w_out) if ctx_out else None
    return y_x, y_c

def peer_block(h, w_query, sub_keys, expert_u, expert_v):
    t = h.shape[0]
    q = (h @ w_query).reshape(t, PEER_HEADS, 2, PEER_KEY_DIM // 2)
    scores = jnp.einsum('thpd,hpnd->thpn', q, sub_keys).astype(jnp.float32)
    top_s, top_i = lax.top_k(scores, PEER_TOPK)
    cand_s = top_s[:, :, 0, :, None] + top_s[:, :, 1, None, :]
    cand_i = top_i[:, :, 0, :, None] * PEER_N_KEYS + top_i[:, :, 1, None, :]
    best_s, best_j = lax.top_k(cand_s.reshape(t, PEER_HEADS, PEER_TOPK * PEER_TOPK), PEER_TOPK)
    expert_idx = jnp.take_along_axis(cand_i.reshape(t, PEER_HEADS, PEER_TOPK * PEER_TOPK), best_j, axis=-1)
    gate = jax.nn.softmax(best_s, axis=-1)
    act = jax.nn.gelu(jnp.einsum('td,thkd->thk', h, expert_u[expert_idx]).astype(jnp.float32),
                      approximate=False)
    coef = (gate * act).astype(h.dtype)
    return jnp.einsum('thk,thkd->td', coef, expert_v[expert_idx])

def peer(h, w_query, sub_keys, expert_u, expert_v):
    blocks = h.reshape(-1, PEER_TOKEN_BLOCK, D_MODEL)
    out = lax.map(lambda hb: peer_block(hb, w_query, sub_keys, expert_u, expert_v), blocks)
    return out.reshape(h.shape)

def setup_inputs(seed: int = 0) -> dict:
    key = jax.random.key(seed)
    ks = jax.random.split(key, 20)

    def nrm(k, shape, s):
        return jax.random.normal(k, shape, jnp.float32) * s

    dir_shape = (DEPTH, N_DIR, DN_HEADS)
    dt = jnp.exp(jax.random.uniform(ks[9], dir_shape, jnp.float32, math.log(1e-3), math.log(1e-1)))
    return {
        'x': nrm(ks[0], (BATCH, SEQ, D_MODEL), 1.0),
        'c': nrm(ks[1], (BATCH, D_MODEL), 1.0),
        'ctx': nrm(ks[2], (BATCH, CTX_LEN, D_MODEL), 1.0),
        'c_ctx': nrm(ks[3], (D_MODEL,), 1.0),
        'w_ada': nrm(ks[4], (DEPTH, D_MODEL, N_MOD * D_MODEL), 0.5 * D_MODEL ** -0.5),
        'b_ada': nrm(ks[5], (DEPTH, N_MOD * D_MODEL), 0.02),
        'w_in': nrm(ks[6], (DEPTH, D_MODEL, IN_COLS), D_MODEL ** -0.5),
        'conv_w': nrm(ks[7], (DEPTH, SHORT_CONV, 3 * DN_WIDTH), SHORT_CONV ** -0.5),
        'a_log': jnp.log(jax.random.uniform(ks[8], dir_shape, jnp.float32, 1.0, 16.0)),
        'dt_bias': dt + jnp.log(-jnp.expm1(-dt)),
        'dn_norm_w': 1.0 + nrm(ks[10], (DEPTH, DN_HEAD_DIM), 0.02),
        'w_four': nrm(ks[11], (DEPTH, F_WIDTH, D_MODEL), F_WIDTH ** -0.5),
        'w_dn': nrm(ks[12], (DEPTH, DN_WIDTH, D_MODEL), DN_WIDTH ** -0.5),
        'w_out': nrm(ks[13], (DEPTH, D_MODEL, D_MODEL), DEEPNORM_BETA * D_MODEL ** -0.5),
        'ln_g': 1.0 + nrm(ks[14], (DEPTH, 2, D_MODEL), 0.02),
        'ln_b': nrm(ks[15], (DEPTH, 2, D_MODEL), 0.02),
        'peer_w_query': nrm(ks[16], (DEPTH, D_MODEL, PEER_HEADS * PEER_KEY_DIM), D_MODEL ** -0.5),
        'peer_sub_keys': nrm(ks[17], (DEPTH, PEER_HEADS, 2, PEER_N_KEYS, PEER_KEY_DIM // 2),
                             (PEER_KEY_DIM // 2) ** -0.5),
        'peer_u': nrm(ks[18], (DEPTH, PEER_EXPERTS, D_MODEL), D_MODEL ** -0.5),
        'peer_v': nrm(ks[19], (DEPTH, PEER_EXPERTS, D_MODEL), DEEPNORM_BETA * PEER_HEADS ** -0.5),
    }

def reference(x, c, ctx, c_ctx, w_ada, b_ada, w_in, conv_w, a_log, dt_bias, dn_norm_w,
              w_four, w_dn, w_out, ln_g, ln_b, peer_w_query, peer_sub_keys, peer_u, peer_v):
    for l in range(DEPTH):
        ctx_out = l + 1 < DEPTH
        mx = ada_modulation(c, w_ada[l], b_ada[l], N_MOD)[:, :, None, :]
        mc = ada_modulation(c_ctx, w_ada[l], b_ada[l], N_MOD if ctx_out else 2)
        hx = modulate(layer_norm(x), mx[:, 0], mx[:, 1])
        hc = modulate(layer_norm(ctx), mc[0], mc[1])
        y_x, y_c = token_mixer(hx, hc, w_in[l], conv_w[l], a_log[l], dt_bias[l], dn_norm_w[l],
                               w_four[l], w_dn[l], w_out[l], ctx_out)
        x = post_norm(x, mx[:, 2] * y_x, ln_g[l, 0], ln_b[l, 0])
        hx = modulate(layer_norm(x), mx[:, 3], mx[:, 4])
        x = post_norm(x, mx[:, 5] * peer(hx, peer_w_query[l], peer_sub_keys[l], peer_u[l], peer_v[l]),
                      ln_g[l, 1], ln_b[l, 1])
        if ctx_out:
            ctx = post_norm(ctx, mc[2] * y_c, ln_g[l, 0], ln_b[l, 0])
            hc = modulate(layer_norm(ctx), mc[3], mc[4])
            ctx = post_norm(ctx, mc[5] * peer(hc, peer_w_query[l], peer_sub_keys[l], peer_u[l], peer_v[l]),
                            ln_g[l, 1], ln_b[l, 1])
    return x


_drawn_inputs = setup_inputs


def setup_inputs(seed=0):
    import zlib

    import numpy as np

    out = dict(_drawn_inputs(seed))
    spreads = {}
    factors = {'ctx': 8.0,
     'c_ctx': 8.0,
     'b_ada': 6.666,
     'a_log': 5.816,
     'dt_bias': 3.064,
     'dn_norm_w': 8.0}
    for name, (base, spread) in spreads.items():
        noise = np.random.default_rng([zlib.crc32(name.encode()), seed]).standard_normal(out[name].shape)
        drawn = base * np.exp(spread * noise) if base else spread * noise
        out[name] = __import__('jax').numpy.asarray(drawn.astype(out[name].dtype))
    for name, factor in factors.items():
        out[name] = (out[name] * factor).astype(out[name].dtype)
    return out
```

```python
import math
from contextlib import ExitStack

import numpy as np

import concourse.bass as bass
from concourse import mybir

F32 = mybir.dt.float32
F32R = mybir.dt.float32r
U32 = mybir.dt.uint32
ACT = mybir.ActivationFunctionType
ALU = mybir.AluOpType
AX = mybir.AxisListType

P = 128
D = 1024
KB = D // P
SEQ, CTX, GRID_W = 512, 256, 64
LAT = SEQ // P
CT = CTX // P
NCH = CT + LAT
H = 8
NDIR = 2
NU = NCH * NDIR
NG = NU // 4
TAPS = 5
LEVELS = 7
FG = 4
PH, PK, TOPK = 8, 128, 16
NEXP_T = PK
ALPHA = 2.0 ** 0.25
LN_EPS = 1e-6
RMS_EPS = 1e-6
L2_EPS = 1e-6
FAR = -1.0e30
GTOK = 64
TK_N = 24
CD_N, CD_EXP = 56, 48
N_IT = 15

T_HEAD = 0
T_F = T_HEAD + 4 * H
T_FOUR = T_F + FG
T_MERGE = T_FOUR + 4
T_OUT = T_MERGE + 3 * KB
T_QUERY = T_OUT + KB
T_PEER = T_QUERY + 2 * PH
T_ALL = T_PEER + 2 * NEXP_T
RING = 4
RAW = 2
ADA_FIRST = 2 * KB
ADA_ALL = 6 * KB

C_ID = 0
C_U = C_ID + P
C_NEG = C_U + 2 * P
C_LVL = C_NEG + 2 * P
C_ONE = C_LVL + LEVELS * 2 * P
C_IOTA = C_ONE + P
C_DFT = C_IOTA + P
C_ALL = C_DFT + 2 * P


def constants():
    c = np.zeros((P, C_ALL), np.float32)
    r = np.arange(P)
    c[:, C_ID:C_ID + P] = np.eye(P)
    j, i = r[:, None], r[None, :]
    c[:, C_U:C_U + P] = j <= i
    c[:, C_U + P:C_U + 2 * P] = j >= i
    c[:, C_NEG:C_NEG + P] = np.where(j <= i, 0.0, FAR)
    c[:, C_NEG + P:C_NEG + 2 * P] = np.where(j >= i, 0.0, FAR)
    for lv in range(LEVELS):
        s = 1 << lv
        same = (j // (2 * s)) == (i // (2 * s))
        low = same & ((j // s) % 2 == 1) & ((i // s) % 2 == 0)
        c[:, C_LVL + (2 * lv) * P:C_LVL + (2 * lv + 1) * P] = -1.0 * low
        c[:, C_LVL + (2 * lv + 1) * P:C_LVL + (2 * lv + 2) * P] = -1.0 * low.T
    c[:, C_ONE:C_ONE + P] = 1.0
    c[:, C_IOTA:C_IOTA + P] = r[None, :]
    a = 2 * np.pi * ((j * i) % P) / P
    c[:, C_DFT:C_DFT + P] = np.cos(a) / math.sqrt(P)
    c[:, C_DFT + P:] = np.sin(a) / math.sqrt(P)
    t = np.arange(SEQ)
    b = 2 * np.pi * ((t[:, None] * t[None, :]) % SEQ) / SEQ
    dft = np.stack([np.cos(b) / math.sqrt(SEQ), -np.sin(b) / math.sqrt(SEQ)])
    dft = dft.reshape(2, LAT, P, SEQ).transpose(2, 0, 1, 3).astype(np.float32)
    return c, np.ascontiguousarray(dft)


def bc(ap, n):
    shape = [int(s) for s in ap.shape]
    return ap.unsqueeze(len(shape)).to_broadcast([*shape, n])


def rep(ap, n):
    shape = [int(s) for s in ap.shape]
    return ap.unsqueeze(1).to_broadcast([shape[0], n, *shape[1:]])


class Map:

    def __init__(self, nc, at, end):
        self.nc, self.at, self.end = nc, at, end

    def branch(self):
        return Map(self.nc, self.at, self.end)

    def __call__(self, name, shape, dt=F32):
        t = self.nc.alloc_sbuf_tensor_at(name, [P, *shape], dt, offset=self.at)
        self.at += (4 * int(np.prod(shape)) + 31) // 32 * 32
        assert self.at <= self.end, (name, self.at, self.end)
        return t


def layer_kernel(nc, A, dbg=None):
    stack = ExitStack()
    with stack:
        def sem(name):
            return stack.enter_context(nc.semaphore(name))

        def sems(name, n):
            return [sem(f"{name}{i}") for i in range(n)]

        bank = [stack.enter_context(nc.psum_tensor(f"bank{i}", [P, 512], F32)) for i in range(8)]

        buf = Map(nc, (nc.sbuf_base + 31) // 32 * 32, nc.sbuf_usable_end)
        cst = buf("cst", [C_ALL])
        raw = buf("raw", [RAW, KB * P])
        w_hi = buf("w_hi", [RING, KB * P], F32R)
        w_lo = buf("w_lo", [RING, KB * P], F32R)
        lat_hi = buf("lat_hi", [KB, SEQ], F32R)
        lat_lo = buf("lat_lo", [KB, SEQ], F32R)
        mods = buf("mods", [ADA_ALL, 2])
        b_ada = buf("b_ada", [ADA_ALL])
        cond = buf("cond", [KB, 2])
        cond_s = buf("cond_s", [KB, 2])
        stats = buf("stats", [NCH, 2, 6])
        mv = buf("mv", [NCH, 2])
        vare = buf("vare", [NCH])
        rstd = buf("rstd", [NCH])
        nhalf = buf("nhalf", [16])
        mark = buf("mark", [1])
        ident = cst[:, C_ID:C_ID + P]
        ones = cst[:, C_ONE:C_ONE + P]
        iota = cst[:, C_IOTA:C_IOTA + P]

        def u_dir(d):
            return cst[:, C_U + d * P:C_U + (d + 1) * P]

        def neg_dir(d):
            return cst[:, C_NEG + d * P:C_NEG + (d + 1) * P]

        after = buf.branch()
        dn = buf("dn", [H, SEQ])
        fou = buf.branch()
        ctx_hi = buf("ctx_hi", [KB, CTX], F32R)
        ctx_lo = buf("ctx_lo", [KB, CTX], F32R)
        ada = buf("ada", [2, KB * P])
        beta = buf("beta", [H * NU])
        gall = buf("gall", [H * NU])
        gcum = buf("gcum", [H * NU])
        kds = buf("kds", [H * NU])
        egl = buf("egl", [H * NU])
        cw = buf("cw", [TAPS, 3 * H])
        nrm_w = buf("nrm_w", [1])

        inp = buf.branch()
        xin = inp("xin", [NCH, D])
        hm = inp("hm", [2, NCH * P])
        ab_w = inp("ab_w", [KB, 32])
        ab_hi = inp("ab_hi", [KB, 32], F32R)
        ab_lo = inp("ab_lo", [KB, 32], F32R)
        dtb = inp("dtb", [16])
        alog = inp("alog", [16])
        expa = inp("expa", [16])
        sp = [inp(f"sp{i}", [H * NU]) for i in range(18)]

        cv = buf("cv", [2, SEQ])
        kT = buf("kT", [NCH * P])
        vT = buf("vT", [NCH * P])
        qT = buf("qT", [SEQ])
        szT = buf("szT", [SEQ])
        rr = buf("rr", [2, 16])
        rn = buf("rn", [16])
        ro = buf("ro", [4])
        rno = buf("rno", [4])
        Kn = buf("Kn", [NCH, P])
        Qn = buf("Qn", [LAT, P])
        Vt = buf("Vt", [NCH, P])
        knT = buf("knT", [NCH * P])
        qnT = buf("qnT", [SEQ])
        gX = buf("gX", [NU, P])
        eN = buf("eN", [NU, P])
        dY = buf("dY", [NU, P])
        Lt = buf("Lt", [NU, P])
        att = buf("att", [2, NDIR, 2 * P])
        kTs = buf("kTs", [NU, P])
        qTs = buf("qTs", [2, NDIR, 2 * P])
        Kd = buf("Kd", [NU, P])
        Rd = buf("Rd", [NDIR, P])
        Vn = buf("Vn", [NDIR, P])
        St = buf("St", [NDIR, 2, P])
        gst = gX
        sqv = Lt[:, :, :].rearrange("p a b -> p (a b)")
        rst = kT[:, 0:LAT * P].rearrange("p (a b) -> p a b", a=LAT)
        rbc = qT
        onT = vT[:, 0:SEQ]

        fy_hi = ctx_hi[:, :, :].rearrange("p a b -> p (a b)").rearrange("p (a b) -> p a b", a=FG)
        fy_lo = ctx_lo[:, :, :].rearrange("p a b -> p (a b)").rearrange("p (a b) -> p a b", a=FG)
        fou.at += 4 * 2 * KB * CTX
        fourT = fou("fourT", [KB, SEQ])
        mer = fou.branch()
        fT = fou("fT", [FG, SEQ])
        fab = fou("fab", [FG, LAT, 2 * P])
        dft = fou("dft", [2, LAT, SEQ])

        low = after.branch()
        low.at += 4 * H * SEQ
        sg = low("sg", [2, SEQ])
        ma = low("ma", [3, SEQ])
        assert low.at <= mer.at - 4 * KB * SEQ
        dn_hi = mer("dn_hi", [H, SEQ], F32R)
        dn_lo = mer("dn_lo", [H, SEQ], F32R)
        mg_hi = mer("mg_hi", [KB, SEQ], F32R)
        mg_lo = mer("mg_lo", [KB, SEQ], F32R)

        x1 = after("x1", [LAT, D])
        pst = after.branch()
        yT = pst("yT", [KB, SEQ])
        gb = pst("gb", [2, D])
        h2 = pst("h2", [2, SEQ])
        xn = pst("xn", [LAT, D])
        pst_end = pst.at

        eidx = after("eidx", [3, P])
        eidT = after("eidT", [3, SEQ])
        keys = after.branch()
        sk = keys("sk", [2 * PH, P])
        qq = keys("qq", [RING, SEQ])
        sc = keys("sc", [2, LAT, P])
        sc2 = keys("sc2", [LAT, P])
        t16 = keys("t16", [RING, LAT, TOPK])
        i16 = keys("i16", [RING, LAT, TOPK], U32)
        topv = keys("topv", [2 * PH, LAT, TOPK])
        topi = keys("topi", [2 * PH, LAT, TOPK])
        cand = keys("cand", [PH, TOPK * TOPK])
        cand2 = keys("cand2", [PH, TOPK * TOPK])
        bs = keys("bs", [PH, TOPK])
        bj = keys("bj", [PH, TOPK], U32)
        bja = keys("bja", [PH, TOPK], U32)
        bjc = keys("bjc", [PH, TOPK], U32)
        bf = [keys(f"bf{i}", [PH, TOPK]) for i in range(8)]
        hot = [keys(f"hot{i}", [PH, TOPK, TOPK]) for i in range(2)]
        pick = keys("pick", [PH, TOPK, TOPK])
        gates = after.branch()
        oh = gates("oh", [2, 4, 2, P])
        gs = gates("gs", [2, P, GTOK])

        g_dram = nc.dram_tensor("g_dram", (SEQ // GTOK, P, PK, GTOK), F32, kind="Internal").ap()

        acc = after("acc", [KB, SEQ])
        c_hi = after("c_hi", [4, SEQ], F32R)
        c_lo = after("c_lo", [4, SEQ], F32R)
        cf = after("cf", [2, SEQ])
        gl = after("gl", [2, SEQ])
        gq = after("gq", [2, SEQ // GTOK, 4, GTOK])
        gb2 = after("gb2", [2, D])
        xo = after("xo", [LAT, D])

        ld_cst, ld_cond, ld_ab, ld_head = sem("ld_cst"), sem("ld_cond"), sem("ld_ab"), sem("ld_head")
        ld_x = sems("ld_x", NCH)
        raw_full = sems("raw_full", RAW)
        ada_full = sems("ada_full", 2)
        hi_done = sem("hi_done")
        split_done = sem("split_done")
        w_used = sem("w_used")
        nhalf_set = sem("nhalf_set")
        cond_done = sem("cond_done")
        ada_mm = sem("ada_mm")
        mods_done = sem("mods_done")
        ln_stat = sem("ln_stat")
        ln_agg = sem("ln_agg")
        ln_var = sem("ln_var")
        ln_rstd = sem("ln_rstd")
        ln_out = sem("ln_out")
        hin_tr = sem("hin_tr")
        hin_mod = sem("hin_mod")
        hin_hi = sem("hin_hi")
        hin_lo = sem("hin_lo")
        ab_split = sem("ab_split")
        ab_mm = sem("ab_mm")
        gate_step = sem("gate_step")
        gate_act = sem("gate_act")
        cum_mm = sem("cum_mm")
        gate_done = sem("gate_done")
        proj = sem("proj")
        conv_tap = sem("conv_tap")
        conv = sem("conv")
        silu = sem("silu")
        z_done = sem("z_done")
        sq_done = sem("sq_done")
        ssq = sem("ssq")
        rr_done = sem("rr_done")
        rn_done = sem("rn_done")
        tr = sem("tr")
        kn = sem("kn")
        trb = sem("trb")
        knt = sem("knt")
        vev = sem("vev")
        gst_done = sem("gst_done")
        gbc = sem("gbc")
        egc = sem("egc")
        dm = sem("dm")
        edm = sem("edm")
        kd_done = sem("kd_done")
        kts = sem("kts")
        kk = sem("kk")
        lt = sem("lt")
        att_done = sem("att_done")
        n1 = sem("n1")
        nn = sem("nn")
        xy = sem("xy")
        x_done = sem("x_done")
        y_done = sem("y_done")
        ks = sem("ks")
        res = sem("res")
        solve = sem("solve")
        vn = sem("vn")
        kdv = sem("kdv")
        state = sem("state")
        o_done = sem("o_done")
        sqo = sem("sqo")
        ssqo = sem("ssqo")
        ro_done = sem("ro_done")
        rno_done = sem("rno_done")
        rst_done = sem("rst_done")
        rbc_mm = sem("rbc_mm")
        rbc_done = sem("rbc_done")
        on_done = sem("on_done")
        dn_done = sem("dn_done")
        ld_dft, ld_res, ld_gb, ld_sk = sem("ld_dft"), sem("ld_res"), sem("ld_gb"), sem("ld_sk")
        f_mm = sem("f_mm")
        f_ev = sem("f_ev")
        fab_mm = sem("fab_mm")
        fab_ev = sem("fab_ev")
        fy_mm = sem("fy_mm")
        fy_h = sem("fy_h")
        fy_l = sem("fy_l")
        four_mm = sem("four_mm")
        four_ev = sem("four_ev")
        dnh = sem("dnh")
        dnl = sem("dnl")
        mer_mm = sem("mer_mm")
        sig = sem("sig")
        mer_v = sem("mer_v")
        mgh = sem("mgh")
        mgl = sem("mgl")
        out_mm = sem("out_mm")
        yt_done = sem("yt_done")
        ytr = sem("ytr")
        x1_sum = sem("x1_sum")
        ln_gain = sem("ln_gain")
        ln_bias = sem("ln_bias")
        h2_tr = sem("h2_tr")
        h2_mod = sem("h2_mod")
        h2_hi = sem("h2_hi")
        h2_lo = sem("h2_lo")
        q_mm = sem("q_mm")
        q_ev = sem("q_ev")
        s_mm = sem("s_mm")
        s_ev = sem("s_ev")
        tk = sem("tk")
        tk_out = sem("tk_out")
        cd = sem("cd")
        cd_exp = sem("cd_exp")
        cd_out = sem("cd_out")
        e_tr = sem("e_tr")
        e_ev = sem("e_ev")
        oh_done = sem("oh_done")
        g_mm = sem("g_mm")
        g_ev = sem("g_ev")
        gs_st = sems("gs_st", 2)
        gq_full = sems("gq_full", 2)
        acc_zero = sem("acc_zero")
        a_mm = sem("a_mm")
        gelu = sem("gelu")
        cf_done = sem("cf_done")
        ch = sem("ch")
        cl = sem("cl")
        v_mm = sem("v_mm")
        acc_done = sem("acc_done")
        fin = sem("fin")
        fin_tr = sem("fin_tr")
        xo_sum = sem("xo_sum")
        st_out = sem("st_out")
        dbg_st = sem("dbg_st")

        def units(t):
            return t[:, :, :].rearrange("p (g d c) n -> p g d c n", g=NG, d=NDIR)

        def unit(d, chunk):
            return (chunk // 2) * 4 + d * 2 + chunk % 2

        def walk(d):
            return [*range(NCH)] if d == 0 else [*range(CT - 1, -1, -1), *range(NCH - 1, CT - 1, -1)]

        def per_head(t, h):
            return t[:, bass.ds(h * NU, NU)]

        def mm3(out, hi, lo, rh, rl, start, stop):
            nc.tensor.matmul(out, hi, rh, start=start, stop=False)
            nc.tensor.matmul(out, hi, rl, start=False, stop=False)
            return nc.tensor.matmul(out, lo, rh, start=False, stop=stop)

        def w_block(slot, k):
            c = slice(k * P, (k + 1) * P)
            return w_hi[:, slot, c], w_lo[:, slot, c]

        block = stack.enter_context(nc.Block())

        @block.sync
        def _(sp_):
            def load_w(n, slot):
                sp_.dma_start(raw[:, slot, :], A["w"][n]).then_inc(raw_full[slot], 16)

            def load_ada(m, slot):
                sp_.dma_start(ada[:, slot, :], A["w_ada"][m]).then_inc(ada_full[slot], 16)

            sp_.dma_start(cond[:, :, :], A["cond"]).then_inc(ld_cond, 16)
            sp_.dma_start(b_ada[:, :], A["b_ada"]).then_inc(ld_cond, 16)
            load_ada(0, 0)
            load_ada(1, 1)
            for t in range(NCH):
                src = A["ctx"][t * P:(t + 1) * P, :] if t < CT else A["x"][(t - CT) * P:(t - CT + 1) * P, :]
                sp_.dma_start(xin[:, t, :], src).then_inc(ld_x[t], 16)
            sp_.dma_start(cst[:, :], A["cst"]).then_inc(ld_cst, 16)
            sp_.dma_start(ab_w[:, :, :], A["ab_w"]).then_inc(ld_ab, 16)
            sp_.dma_start(dtb[:, :], A["dtb"].partition_broadcast(P)).then_inc(ld_ab, 16)
            sp_.dma_start(alog[:, :], A["alog"].partition_broadcast(P)).then_inc(ld_ab, 16)
            sp_.dma_start(cw[:, :, :], A["cw"]).then_inc(ld_head, 16)
            sp_.dma_start(nrm_w[:, :], A["nrm_w"]).then_inc(ld_head, 16)
            load_w(0, 0)
            load_w(1, 1)
            with sp_.Fori(1, ADA_FIRST // 2) as i:
                for j in range(2):
                    sp_.wait_ge(ada_mm, i * 2 + (j - 1))
                    load_ada(i * 2 + j, j)
            with sp_.Fori(0, H) as h:
                for j in range(4):
                    sp_.wait_ge(split_done, h * 4 + (j + 1))
                    load_w(h * 4 + (j + 2), j % 2)
                    sp_.wait_ge(ada_mm, h * 4 + (ADA_FIRST + j - 1))
                    load_ada(h * 4 + (ADA_FIRST + j), j % 2)
            with sp_.Fori(0, (T_PEER - T_F - 2) // 2) as i:
                for j in range(2):
                    sp_.wait_ge(split_done, i * 2 + (T_F + 1 + j))
                    load_w(i * 2 + (T_F + 2 + j), j)
            for j in range(RING):
                sp_.wait_ge(split_done, T_PEER - 1 + j)
                load_w(T_PEER + j, j % RAW)
            with sp_.Fori(0, SEQ // GTOK // 2) as i:
                for j in range(2):
                    sp_.wait_ge(g_ev, i * (2 * GTOK // 4) + (j + 1) * (GTOK // 4))
                    sp_.dma_start(g_dram[i * 2 + j], gs[:, j, :, :]).then_inc(gs_st[j], 16)
            for j in range(2):
                sp_.wait_ge(gs_st[j], SEQ // GTOK // 2 * 16)

            def load_gq(q, slot):
                sp_.dma_start(gq[:, slot, :, :, :].rearrange("p g i t -> p g (i t)"),
                              g_dram.rearrange("g j (q i) t -> q j g (i t)", i=4)[q]).then_inc(gq_full[slot], 16)

            def peer_loads(q, base, count):
                for x in range(count):
                    sp_.wait_ge(split_done, base + (x + RING - 1))
                    load_w(base + (x + RING), x % RAW)
                    if x == 7 and count == 16:
                        sp_.wait_ge(cf_done, q * 8 + 4)
                        load_gq(q * 2 + 2, 0)
                sp_.wait_ge(cf_done, q * 8 + 8)
                if count == 16:
                    load_gq(q * 2 + 3, 1)

            load_gq(0, 0)
            load_gq(1, 1)
            with sp_.Fori(0, N_IT) as q:
                peer_loads(q, q * 16 + T_PEER, 16)
            peer_loads(N_IT, N_IT * 16 + T_PEER, 12)
            for b in range(LAT):
                sp_.wait_ge(ln_bias, LAT + b + 1)
                sp_.dma_start(A["out"][b * P:(b + 1) * P, :], xo[:, b, :]).then_inc(st_out, 16)
            sp_.wait_ge(st_out, LAT * 16)
            if dbg:
                for n_, t_ in (("x1", x1[:, :, :]), ("eidT", eidT[:, :, :]), ("lat_hi", lat_hi[:, :, :].bitcast(F32)),
                               ("acc", acc[:, :, :])):
                    sp_.dma_start(dbg[n_], t_).then_inc(dbg_st, 16)
                sp_.wait_ge(dbg_st, 64)

        @block.scalar
        def _(act):
            def hi(n, i, m, slot):
                act.wait_ge(raw_full[slot % RAW], (i * m[0] + m[1]) * 16)
                nc.scalar.copy(w_hi[:, slot, :], raw[:, slot % RAW, :]).then_inc(hi_done, 1)

            act.wait_ge(ld_cond, 32)
            nc.scalar.activation(cond_s[:, :, :], cond[:, :, :], ACT.Silu).then_inc(cond_done, 1)
            act.wait_ge(ld_ab, 48)
            nc.scalar.copy(ab_hi[:, :, :], ab_w[:, :, :]).then_inc(ab_split, 1)
            nc.scalar.activation(expa[:, :], alog[:, :], ACT.Exp).then_inc(gate_act, 1)
            act.wait_ge(mods_done, 2)
            for k in range(KB):
                act.wait_ge(hin_tr, k + 1)
                if k >= 2:
                    act.wait_ge(hin_lo, 2 * (k - 1))
                for s, (src, n0, n1_) in enumerate(((bank[k % 2][:, :], CTX, CTX + SEQ),
                                                    (bank[2 + k % 2][:, 0:CTX], 0, CTX))):
                    nc.scalar.activation(hm[:, k % 2, n0:n1_], src, ACT.Identity, bias=mods[:, k, s:s + 1],
                                         scale=mods[:, KB + k, s:s + 1]).then_inc(hin_mod, 1)
                act.wait_ge(hin_mod, 2 * k + 2)
                nc.scalar.copy(lat_hi[:, k, :], hm[:, k % 2, CTX:]).then_inc(hin_hi, 1)
                nc.scalar.copy(ctx_hi[:, k, :], hm[:, k % 2, 0:CTX]).then_inc(hin_hi, 1)
            for j in range(RING):
                hi(j, 0, (0, j // 2 + 1), j)
            act.wait_ge(gate_step, 5)
            nc.scalar.activation(sp[3][:, :], sp[2][:, :], ACT.Exp).then_inc(gate_act, 1)
            nc.scalar.activation(sp[4][:, :], sp[1][:, :], ACT.Exp, scale=-1.0).then_inc(gate_act, 1)
            act.wait_ge(gate_done, 4)
            nc.scalar.activation(kds[:, :], sp[17][:, :], ACT.Exp).then_inc(gate_act, 1)
            act.wait_ge(cum_mm, 3)
            nc.scalar.activation(egl[:, :], bank[5][:, H * NU:2 * H * NU], ACT.Exp).then_inc(gate_act, 1)

            with act.Fori(0, H) as h:
                for o, (dst, a, b) in enumerate(((kT, CTX, CTX + SEQ), (kT, 0, CTX),
                                                 (vT, CTX, CTX + SEQ), (vT, 0, CTX), (qT, 0, SEQ))):
                    act.wait_ge(conv, h * 5 + (o + 1))
                    nc.scalar.activation(dst[:, a:b], cv[:, o % 2, 0:b - a], ACT.Silu).then_inc(silu, 1)
                    if o in (1, 3, 4):
                        j = o // 2
                        hi(None, h, (2, 3 + j // 2), j)
                act.wait_ge(dn_done, h)
                act.wait_ge(proj, h * 6 + 6)
                nc.scalar.activation(szT[:, :], bank[1][:, :], ACT.Silu).then_inc(z_done, 1)
                hi(None, h, (2, 4), 3)
                act.wait_ge(silu, h * 5 + 2)
                nc.scalar.activation(sqv[:, 0:NCH * P], kT[:, :], ACT.Square).then_inc(sq_done, 1)
                act.wait_ge(silu, h * 5 + 5)
                nc.scalar.activation(sqv[:, NCH * P:NCH * P + SEQ], qT[:, :], ACT.Square).then_inc(sq_done, 1)
                act.wait_ge(tr, h * 3 + 3)
                nc.scalar.copy(Vt[:, 0:4, :].rearrange("p a b -> p (a b)"), bank[5][:, :]).then_inc(vev, 1)
                nc.scalar.copy(Vt[:, 4:6, :].rearrange("p a b -> p (a b)"), bank[6][:, 0:CTX]).then_inc(vev, 1)
                act.wait_ge(trb, h * 2 + 1)
                nc.scalar.copy(knT[:, 0:512], bank[2][:, :]).then_inc(knt, 1)
                nc.scalar.copy(knT[:, 512:], bank[3][:, 0:CTX]).then_inc(knt, 1)
                act.wait_ge(trb, h * 2 + 2)
                nc.scalar.copy(qnT[:, :], bank[4][:, :]).then_inc(knt, 1)
                for g in range(NG):
                    act.wait_ge(gbc, h * 3 + (g + 1))
                    nc.scalar.activation(eN[:, 4 * g:4 * g + 4, :].rearrange("p a b -> p (a b)"), bank[5 + g][:, :],
                                         ACT.Exp).then_inc(egc, 1)
                for g in range(NG):
                    act.wait_ge(dm, h * 12 + 4 * (g + 1))
                    v = dY[:, 4 * g:4 * g + 4, :].rearrange("p a b -> p (a b)")
                    nc.scalar.activation(v, v, ACT.Exp).then_inc(edm, 1)
                act.wait_ge(o_done, h + 1)
                nc.scalar.activation(sqv[:, 0:SEQ], bank[2][:, :], ACT.Square).then_inc(sqo, 1)
                act.wait_ge(rbc_mm, h + 1)
                nc.scalar.copy(rbc[:, :], bank[4][:, :]).then_inc(rbc_done, 1)

            def hi_n(q, i=0, per=0):
                act.wait_ge(raw_full[q % RAW], i * (per // 2 * 16) + (q // 2 + 1) * 16)
                nc.scalar.copy(w_hi[:, q % RING, :], raw[:, q % RAW, :]).then_inc(hi_done, 1)

            act.wait_ge(dn_done, H)
            act.dma_start(dft[:, :, :, :], A["dft"]).then_inc(ld_dft, 16)
            for m in range(FG):
                act.wait_ge(f_mm, m + 1)
                nc.scalar.copy(fT[:, m, :], bank[m % 2][:, :]).then_inc(f_ev, 1)
                hi_n(T_F + RING + m)
            for m in range(FG):
                act.wait_ge(fy_mm, m + 1)
                nc.scalar.copy(fy_hi[:, m, :], bank[6 + m % 2][:, :]).then_inc(fy_h, 1)
            for m in range(H):
                nc.scalar.copy(dn_hi[:, m, :], dn[:, m, :]).then_inc(dnh, 1)
            for m in range(KB):
                act.wait_ge(four_mm, m + 1)
                nc.scalar.copy(fourT[:, m, :], bank[m % 2][:, :]).then_inc(four_ev, 1)
                if m % 2:
                    hi_n(T_FOUR + RING + m // 2)
            act.wait_ge(dnl, H)
            act.dma_start(x1[:, :, :], A["x"].rearrange("(b p) n -> p b n", p=P)).then_inc(ld_res, 16)
            with act.Fori(0, 2) as i:
                for m in range(4):
                    for t in range(2):
                        act.wait_ge(mer_v, i * 12 + (3 * m))
                        act.wait_ge(mer_mm, i * 12 + (3 * m + t + 1))
                        nc.scalar.activation(sg[:, t, :], bank[3 * (m % 2) + t][:, :], ACT.Sigmoid).then_inc(sig, 1)
                        hi_n(T_MERGE + RING + 3 * m + t, i, 12)
                    act.wait_ge(mer_v, i * 12 + (3 * m + 3))
                    nc.scalar.copy(mg_hi[:, bass.ds(i * 4 + m, 1), :], ma[:, 2:3, :]).then_inc(mgh, 1)
                    hi_n(T_MERGE + RING + 3 * m + 2, i, 12)
            act.wait_ge(mgl, KB)
            act.dma_start(gb[:, 0, :], A["ln"][0].partition_broadcast(P)).then_inc(ld_gb, 16)
            act.dma_start(gb[:, 1, :], A["ln"][2].partition_broadcast(P)).then_inc(ld_gb, 16)
            for m in range(KB):
                act.wait_ge(out_mm, m + 1)
                nc.scalar.activation(yT[:, m, :], bank[m % 2][:, :], ACT.Copy,
                                     scale=mods[:, 2 * KB + m, 0:1]).then_inc(yt_done, 1)
                hi_n(T_OUT + RING + m)
            for k in range(KB):
                act.wait_ge(h2_tr, k + 1)
                if k >= 2:
                    act.wait_ge(h2_lo, k - 1)
                nc.scalar.activation(h2[:, k % 2, :], bank[k % 2][:, :], ACT.Identity, bias=mods[:, 3 * KB + k, 0:1],
                                     scale=mods[:, 4 * KB + k, 0:1]).then_inc(h2_mod, 1)
                act.wait_ge(h2_mod, k + 1)
                nc.scalar.copy(lat_hi[:, k, :], h2[:, k % 2, :]).then_inc(h2_hi, 1)
            act.wait_ge(h2_lo, KB)
            act.dma_start(sk[:, :, :], A["sub_keys"]).then_inc(ld_sk, 16)
            with act.Fori(0, 2 * PH // 4) as i:
                for j in range(4):
                    act.wait_ge(q_mm, i * 4 + (j + 1))
                    nc.scalar.copy(qq[:, j, :], bank[j % 2][:, :]).then_inc(q_ev, 1)
                    hi_n(T_QUERY + RING + j, i, 4)
                    act.wait_ge(tk, i * (4 * TK_N) + max(TK_N * (j - 1), 0))
                    act.wait_ge(s_mm, i * 4 + (j + 1))
                    nc.scalar.copy(sc[:, j % 2, :, :].rearrange("p a b -> p (a b)"), bank[2 + j % 2][:, :]).then_inc(s_ev, 1)
            with act.Fori(0, LAT) as b:
                act.wait_ge(cd, b * CD_N + CD_EXP)
                nc.scalar.activation(bf[5][:, :, :], bf[4][:, :, :], ACT.Exp).then_inc(cd_exp, 1)
                act.wait_ge(e_tr, b + 1)
                nc.scalar.copy(eidT[:, :, bass.ds(b * P, P)], bank[4][:, 0:3 * P].rearrange("p (a b) -> p a b", a=3)).then_inc(e_ev, 1)
            with act.Fori(0, SEQ // GTOK // 2) as i:
                for j in range(2):
                    act.wait_ge(gs_st[j], i * 16)
                    with act.Fori(0, GTOK // 8) as t:
                        for z in range(2):
                            act.wait_ge(g_mm, i * (2 * GTOK // 4) + t * 2 + (j * GTOK // 4 + z + 1))
                            nc.scalar.copy(gs[:, j, :, bass.ds(t * 8 + 4 * z, 4)].rearrange("p i t -> p t i"),
                                           bank[z][:, :].rearrange("p (t i) -> p t i", t=4)).then_inc(g_ev, 1)
            def act_gelu(i, loc):
                act.wait_ge(a_mm, i + (loc + 1))
                if loc >= 2:
                    act.wait_ge(cf_done, i + (loc - 1))
                nc.scalar.activation(gl[:, loc % 2, :], bank[loc % 2][:, :], ACT.Gelu).then_inc(gelu, 1)

            def act_c(i, loc):
                act.wait_ge(cf_done, i + (loc + 1))
                nc.scalar.copy(c_hi[:, loc % 4, :], cf[:, loc % 2, :]).then_inc(ch, 1)

            def act_pairs(q, i, per, n_pair, last):
                for r_ in range(n_pair):
                    n0 = T_PEER + 2 + 4 * r_ + RING
                    end = last and r_ == n_pair - 1
                    tail = last and r_ == n_pair - 2
                    if not end:
                        act_gelu(i, 2 * r_ + 2)
                        hi_n(n0, q, per)
                        act_c(i, 2 * r_ + 2)
                        act.wait_ge(v_mm, i * 4 + 8 * (r_ + 1))
                        hi_n(n0 + 1, q, per)
                        if not tail:
                            hi_n(n0 + 2, q, per)
                        act_gelu(i, 2 * r_ + 3)
                        if not tail:
                            hi_n(n0 + 3, q, per)
                        act_c(i, 2 * r_ + 3)

            for j in range(2):
                act.wait_ge(gs_st[j], SEQ // GTOK // 2 * 16)
            act.dma_start(gb2[:, 0, :], A["ln"][1].partition_broadcast(P)).then_inc(ld_gb, 16)
            act.dma_start(gb2[:, 1, :], A["ln"][3].partition_broadcast(P)).then_inc(ld_gb, 16)
            for j in range(2):
                act_gelu(0, j)
                hi_n(T_PEER + RING + j)
                act_c(0, j)
            with act.Fori(0, N_IT) as q:
                act_pairs(q, q * 8, 16, 4, False)
            act_pairs(N_IT, N_IT * 8, 16, 4, True)
            act.wait_ge(acc_done, 4 * PK)
            for k in range(KB):
                nc.scalar.activation(acc[:, k, :], acc[:, k, :], ACT.Copy, scale=mods[:, 5 * KB + k, 0:1]).then_inc(fin, 1)

        @block.gpsimd
        def _(pool):
            def lo(slot, *count):
                pool.wait_ge(hi_done, *count)
                nc.gpsimd.tensor_sub(w_lo[:, slot, :], raw[:, slot % RAW, :],
                                     w_hi[:, slot, :].bitcast(F32)).then_inc(split_done, 1)

            nc.gpsimd.memset(nhalf[:, :], -0.5).then_inc(nhalf_set, 1)
            pool.wait_ge(nhalf_set, 1)
            pool.wait_ge(ln_var, 1)
            nc.gpsimd.tensor_tensor(rstd[:, :], vare[:, :], nhalf[:, 0:NCH], ALU.pow).then_inc(ln_rstd, 1)
            for j in range(RING):
                lo(j, j + 1)
            with pool.Fori(0, H) as h:
                for j in range(4):
                    lo(j, h * 4 + (5 + j))
                pool.wait_ge(rr_done, h * 2 + 2)
                nc.gpsimd.tensor_tensor(rn[:, 0:NCH + LAT], rr[:, 0, 0:NCH + LAT], nhalf[:, 0:NCH + LAT],
                                        ALU.pow).then_inc(rn_done, 1)
                pool.wait_ge(dn_done, h)
                pool.wait_ge(gate_done, 5)
                nc.gpsimd.tensor_copy(gst[:, :, :], bc(per_head(gall, h), P)).then_inc(gst_done, 1)
                pool.wait_ge(kn, h * 3 + 2)
                for d in range(NDIR):
                    scale = per_head(kds, h).rearrange("p (g d c) -> p g d c", g=NG, d=NDIR)[:, :, d, :]
                    nc.gpsimd.tensor_mul(units(Kd)[:, :, d, :, :],
                                         Kn[:, :, :].rearrange("p (g c) n -> p g c n", g=NG),
                                         bc(scale, P)).then_inc(kd_done, 1)
                pool.wait_ge(knt, h * 3 + 2)
                pool.wait_ge(egc, h * 3 + 3)
                e4 = eN[:, :, :].rearrange("p (g d c) n -> p g d (c n)", g=NG, d=NDIR)
                k4 = kTs[:, :, :].rearrange("p (g d c) n -> p g d (c n)", g=NG, d=NDIR)
                for d in range(NDIR):
                    nc.gpsimd.tensor_mul(k4[:, :, d, :], knT[:, :].rearrange("p (g n) -> p g n", g=NG),
                                         e4[:, :, d, :]).then_inc(kts, 1)
                pool.wait_ge(knt, h * 3 + 3)
                for d in range(NDIR):
                    nc.gpsimd.tensor_mul(qTs[:, :, d, :], qnT[:, :].rearrange("p (g n) -> p g n", g=2),
                                         e4[:, 1:NG, d, :]).then_inc(kts, 1)
                pool.wait_ge(ro_done, h + 1)
                nc.gpsimd.tensor_tensor(rno[:, :], ro[:, :], nhalf[:, 0:LAT], ALU.pow).then_inc(rno_done, 1)
                pool.wait_ge(rno_done, h + 1)
                nc.gpsimd.tensor_mul(rst, bc(rno[:, :], P), rep(ones, LAT)).then_inc(rst_done, 1)

            with pool.Fori(0, (T_QUERY - T_F) // 4) as i:
                for j in range(4):
                    lo(j, i * 4 + (T_F + RING + 1 + j))
            for n_norm in (1, 2):
                pool.wait_ge(ln_var, n_norm + 1)
                nc.gpsimd.tensor_tensor(rstd[:, 0:LAT], vare[:, 0:LAT], nhalf[:, 0:LAT], ALU.pow).then_inc(ln_rstd, 1)
            with pool.Fori(0, (T_ALL - T_QUERY - RING) // 4) as i:
                for j in range(4):
                    lo(j, i * 4 + (T_QUERY + RING + 1 + j))
            pool.wait_ge(ln_var, 4)
            nc.gpsimd.tensor_tensor(rstd[:, 0:LAT], vare[:, 0:LAT], nhalf[:, 0:LAT], ALU.pow).then_inc(ln_rstd, 1)

        @block.vector
        def _(dve):
            steps = [0]

            def link(ins):
                steps[0] += 1
                ins.then_inc(gate_step, 1)
                dve.wait_ge(gate_step, steps[0])

            for t in range(NCH):
                dve.wait_ge(ld_x[t], 16)
                for i in range(2):
                    nc.vector.bn_stats(stats[:, t, i, :], xin[:, t, i * 512:(i + 1) * 512]).then_inc(ln_stat, 1)
            for t in range(NCH):
                dve.wait_ge(ln_stat, 2 * t + 2)
                nc.vector.bn_aggr(mv[:, t, :], stats[:, t, :, :]).then_inc(ln_agg, 1)
            dve.wait_ge(ln_agg, NCH)
            nc.vector.tensor_scalar(vare[:, :], mv[:, :, 1], LN_EPS, None, ALU.add).then_inc(ln_var, 1)
            dve.wait_ge(ln_rstd, 1)
            for t in range(NCH):
                nc.vector.tensor_scalar(xin[:, t, :], xin[:, t, :], mv[:, t, 0:1], rstd[:, t:t + 1],
                                        ALU.subtract, ALU.mult).then_inc(ln_out, 1)
            dve.wait_ge(ada_mm, ADA_FIRST)
            nc.vector.tensor_tensor(mods[:, 0:ADA_FIRST, :],
                                    bank[7][:, 0:2 * ADA_FIRST].rearrange("p (a b) -> p a b", b=2),
                                    bc(b_ada[:, 0:ADA_FIRST], 2), ALU.add).then_inc(mods_done, 1)
            dve.wait_ge(mods_done, 1)
            nc.vector.tensor_scalar(mods[:, KB:2 * KB, :], mods[:, KB:2 * KB, :], 1.0, None,
                                    ALU.add).then_inc(mods_done, 1)
            dve.wait_ge(ab_split, 1)
            nc.vector.tensor_sub(ab_lo[:, :, :], ab_w[:, :, :], ab_hi[:, :, :].bitcast(F32)).then_inc(ab_split, 1)
            for k in range(KB):
                dve.wait_ge(hin_hi, 2 * k + 2)
                nc.vector.tensor_sub(lat_lo[:, k, :], hm[:, k % 2, CTX:],
                                     lat_hi[:, k, :].bitcast(F32)).then_inc(hin_lo, 1)
                nc.vector.tensor_sub(ctx_lo[:, k, :], hm[:, k % 2, 0:CTX],
                                     ctx_hi[:, k, :].bitcast(F32)).then_inc(hin_lo, 1)
            dve.wait_ge(ab_mm, 1)
            dve.wait_ge(ld_ab, 48)
            abp = bank[4][:, 0:NCH * 32].rearrange("p (g c e d h) -> p e d h g c", g=NG, c=2, e=2, d=NDIR)

            def gv(t):
                return t[:, :].rearrange("p (h g d c) -> p d h g c", h=H, g=NG, d=NDIR)

            def over_units(t, d):
                return bc(bc(t[:, d * H:(d + 1) * H], NG), 2)

            for d in range(NDIR):
                nc.vector.tensor_tensor(gv(sp[0])[:, d], abp[:, 0, d], over_units(dtb, d), ALU.add).then_inc(gate_step, 1)
                nc.vector.tensor_copy(gv(sp[1])[:, d], abp[:, 1, d]).then_inc(gate_step, 1)
            steps[0] = 4
            dve.wait_ge(gate_step, 4)
            link(nc.vector.scalar_tensor_tensor(sp[2][:, :], sp[0][:, :], -1.0, sp[0][:, :], ALU.mult, ALU.min))
            dve.wait_ge(gate_act, 3)
            link(nc.vector.tensor_scalar(sp[5][:, :], sp[3][:, :], 2.0, None, ALU.add))
            link(nc.vector.reciprocal(sp[6][:, :], sp[5][:, :]))
            link(nc.vector.tensor_tensor(sp[7][:, :], sp[3][:, :], sp[6][:, :], ALU.mult))
            link(nc.vector.tensor_tensor(sp[8][:, :], sp[7][:, :], sp[7][:, :], ALU.mult))
            link(nc.vector.tensor_scalar(sp[9][:, :], sp[8][:, :], 1.0 / 17, None, ALU.mult))
            cur = 9
            for c in (15, 13, 11, 9, 7, 5, 3):
                link(nc.vector.scalar_tensor_tensor(sp[19 - cur][:, :], sp[cur][:, :], 1.0 / c, sp[8][:, :],
                                                    ALU.add, ALU.mult))
                cur = 19 - cur
            link(nc.vector.scalar_tensor_tensor(sp[11][:, :], sp[cur][:, :], 1.0, sp[7][:, :], ALU.add, ALU.mult))
            link(nc.vector.tensor_scalar(sp[12][:, :], sp[0][:, :], 0.0, None, ALU.max))
            link(nc.vector.scalar_tensor_tensor(sp[13][:, :], sp[11][:, :], 2.0, sp[12][:, :], ALU.mult, ALU.add))
            link(nc.vector.tensor_scalar(sp[14][:, :], sp[13][:, :], -1.0, None, ALU.mult))
            for d in range(NDIR):
                nc.vector.tensor_tensor(gv(gall)[:, d], gv(sp[14])[:, d], over_units(expa, d),
                                        ALU.mult).then_inc(gate_done, 1)
            link(nc.vector.tensor_scalar(sp[15][:, :], sp[4][:, :], 1.0, None, ALU.add))
            nc.vector.reciprocal(beta[:, :], sp[15][:, :]).then_inc(gate_done, 1)
            dve.wait_ge(cum_mm, 3)
            link(nc.vector.tensor_copy(gcum[:, :], bank[5][:, 0:H * NU]))
            nc.vector.tensor_tensor(sp[17][:, :], bank[5][:, H * NU:2 * H * NU], gcum[:, :],
                                    ALU.subtract).then_inc(gate_done, 1)
            dve.wait_ge(gate_act, 5)
            dve.wait_ge(ld_head, 32)
            nc.vector.tensor_copy(sp[16][:, :], beta[:, :]).then_inc(gate_done, 1)

            with dve.Fori(0, H) as h:
                for o in range(5):
                    kind, lat = o // 2, o % 2 == 0
                    n_row, row = (SEQ // GRID_W, GRID_W) if lat else (1, CTX)
                    src = bank[o % 2][:, 0:n_row * row].rearrange("p (r n) -> p r n", r=n_row)
                    dst = cv[:, o % 2, 0:n_row * row].rearrange("p (r n) -> p r n", r=n_row)
                    dve.wait_ge(silu, h * 5 + max(o - 1, 0))
                    dve.wait_ge(proj, h * 6 + (o + 1))

                    def tap(t):
                        return cw[:, t, bass.ds(h + kind * H, 1)]

                    nc.vector.tensor_scalar(dst, src, tap(TAPS // 2), None, ALU.mult).then_inc(conv_tap, 1)
                    others = [t for t in range(TAPS) if t != TAPS // 2]
                    for n, t in enumerate(others):
                        s = t - TAPS // 2
                        a, b = max(0, -s), row - max(0, s)
                        dve.wait_ge(conv_tap, h * 20 + (4 * o + n + 1))
                        nc.vector.scalar_tensor_tensor(dst[:, :, a:b], src[:, :, a + s:b + s], tap(t), dst[:, :, a:b],
                                                       ALU.mult, ALU.add).then_inc(conv if n == 3 else conv_tap, 1)
                dve.wait_ge(ada_mm, h * 4 + (ADA_FIRST + 4))
                nc.vector.tensor_tensor(mods[:, bass.ds(h * 4 + ADA_FIRST, 4), :],
                                        bank[7][:, 256:264].rearrange("p (a b) -> p a b", b=2),
                                        bc(b_ada[:, bass.ds(h * 4 + ADA_FIRST, 4)], 2), ALU.add).then_inc(mods_done, 1)
                dve.wait_ge(ssq, h + 1)
                nc.vector.tensor_scalar(rr[:, 0, 0:NCH], bank[7][:, 0:NCH], L2_EPS, None, ALU.add).then_inc(rr_done, 1)
                nc.vector.tensor_scalar(rr[:, 0, NCH:NCH + LAT], bank[7][:, NCH:NCH + LAT], float(P), P * L2_EPS,
                                        ALU.mult, ALU.add).then_inc(rr_done, 1)
                dve.wait_ge(tr, h * 3 + 2)
                dve.wait_ge(kd_done, h * 2)
                dve.wait_ge(rn_done, h + 1)
                b4 = "p (a b) -> p a b"
                nc.vector.tensor_tensor(Kn[:, 0:4, :], bank[2][:, :].rearrange(b4, b=P), bc(rn[:, 0:4], P),
                                        ALU.mult).then_inc(kn, 1)
                nc.vector.tensor_tensor(Kn[:, 4:6, :], bank[3][:, 0:CTX].rearrange(b4, b=P), bc(rn[:, 4:6], P),
                                        ALU.mult).then_inc(kn, 1)
                nc.vector.tensor_tensor(Qn[:, :, :], bank[4][:, :].rearrange(b4, b=P), bc(rn[:, 6:10], P),
                                        ALU.mult).then_inc(kn, 1)
                for g in range(NG):
                    dve.wait_ge(egc, h * 3 + (g + 1))
                    for q in range(4):
                        u = 4 * g + q
                        nc.vector.scalar_tensor_tensor(dY[:, u, :], bank[5 + g][:, q * P:(q + 1) * P],
                                                       gcum[:, bass.ds(h * NU + u, 1)], neg_dir(q // 2),
                                                       ALU.subtract, ALU.min).then_inc(dm, 1)
                dve.wait_ge(kk, h * 2 + 1)
                for g in range(NG):
                    dve.wait_ge(edm, h * 3 + (g + 1))
                    for q in range(4):
                        u, c = 4 * g + q, 2 * g + q % 2
                        nc.vector.scalar_tensor_tensor(Lt[:, u, :], bank[2 + c // 4][:, (c % 4) * P:(c % 4 + 1) * P],
                                                       beta[:, bass.ds(h * NU + u, 1)], dY[:, u, :],
                                                       ALU.mult, ALU.mult).then_inc(lt, 1)
                dve.wait_ge(kk, h * 2 + 2)
                d4 = dY[:, :, :].rearrange("p (g d c) n -> p g d (c n)", g=NG, d=NDIR)
                for g in range(2):
                    nc.vector.tensor_tensor(att[:, g, :, :], rep(bank[4][:, g * 256:(g + 1) * 256], NDIR),
                                            d4[:, g + 1, :, :], ALU.mult).then_inc(att_done, 1)

                def masked(h, lv, base):
                    for g in range(NG):
                        dve.wait_ge(n1, base + (g + 1))
                        m = cst[:, bass.ds(lv * (2 * P) + C_LVL, 2 * P)].rearrange("p (d n) -> p d n", d=NDIR)
                        m = m.unsqueeze(2).to_broadcast([P, NDIR, 2, P])
                        nc.vector.tensor_tensor(units(eN)[:, g], bank[2 + g][:, :].rearrange(
                            "p (d c n) -> p d c n", d=NDIR, c=2), m, ALU.mult).then_inc(nn, 1)

                dve.wait_ge(kts, h * 4 + 4)
                masked(h, 0, h * 21)
                id4 = rep(ident, 4)
                for g in range(NG):
                    u4 = slice(4 * g, 4 * g + 4)
                    dve.wait_ge(nn, h * 21 + (g + 1))
                    nc.vector.tensor_tensor(dY[:, u4, :], eN[:, u4, :], id4, ALU.add).then_inc(y_done, 1)
                    dve.wait_ge(xy, h * 21 + (g + 1))
                    nc.vector.tensor_tensor(gX[:, u4, :], bank[5 + g][:, :].rearrange(b4, b=P), id4,
                                            ALU.add).then_inc(x_done, 1)

                def add_up(base, last):
                    for g in range(NG):
                        u4 = slice(4 * g, 4 * g + 4)
                        dve.wait_ge(xy, base + (g + 1))
                        if not last:
                            nc.vector.tensor_tensor(dY[:, u4, :], dY[:, u4, :], bank[2 + g][:, :].rearrange(b4, b=P),
                                                    ALU.add).then_inc(y_done, 1)
                        nc.vector.tensor_tensor(gX[:, u4, :], gX[:, u4, :], bank[5 + g][:, :].rearrange(b4, b=P),
                                                ALU.add).then_inc(x_done, 1)

                with dve.Fori(1, LEVELS - 1) as lv:
                    masked(h, lv, h * 21 + lv * 3)
                    add_up(h * 21 + lv * 3, False)
                masked(h, LEVELS - 1, h * 21 + (LEVELS - 1) * 3)
                add_up(h * 21 + (LEVELS - 1) * 3, True)

                for s in range(NCH):
                    if s:
                        for d in range(NDIR):
                            dve.wait_ge(ks, h * 10 + (2 * (s - 1) + d + 1))
                            nc.vector.tensor_tensor(Rd[:, d, :], Vt[:, walk(d)[s], :], bank[3 + d][:, 0:P],
                                                    ALU.subtract).then_inc(res, 1)
                    for d in range(NDIR):
                        u = unit(d, walk(d)[s])
                        dve.wait_ge(solve, h * 12 + (2 * s + d + 1))
                        nc.vector.tensor_scalar(Vn[:, d, :], bank[5 + d][:, 0:P], beta[:, bass.ds(h * NU + u, 1)],
                                                None, ALU.mult).then_inc(vn, 1)
                    if s < NCH - 1:
                        for d in range(NDIR):
                            u = unit(d, walk(d)[s])
                            dve.wait_ge(kdv, h * 10 + (2 * s + d + 1))
                            new = bank[3 + d][:, 0:P]
                            if s == 0:
                                nc.vector.tensor_copy(St[:, d, 0, :], new).then_inc(state, 1)
                            else:
                                dve.wait_ge(state, h * 10 + (2 * (s - 1) + d + 1))
                                nc.vector.scalar_tensor_tensor(St[:, d, s % 2, :], St[:, d, (s - 1) % 2, :],
                                                               egl[:, bass.ds(h * NU + u, 1)], new,
                                                               ALU.mult, ALU.add).then_inc(state, 1)
                dve.wait_ge(ssqo, h + 1)
                nc.vector.tensor_scalar(ro[:, :], bank[3][:, 0:LAT], 1.0 / P, RMS_EPS, ALU.mult,
                                        ALU.add).then_inc(ro_done, 1)
                dve.wait_ge(rbc_done, h + 1)
                nc.vector.tensor_tensor(onT, bank[2][:, :], rbc[:, :], ALU.mult).then_inc(on_done, 1)
                dve.wait_ge(z_done, h + 1)
                dve.wait_ge(on_done, h + 1)
                nc.vector.scalar_tensor_tensor(dn[:, h, :], onT, nrm_w[:, 0:1], szT[:, :], ALU.mult,
                                               ALU.mult).then_inc(dn_done, 1)

            nc.vector.tensor_scalar(mods[:, 4 * KB:5 * KB, :], mods[:, 4 * KB:5 * KB, :], 1.0, None,
                                    ALU.add).then_inc(mods_done, 1)
            for e in range(2 * FG):
                dve.wait_ge(fab_mm, e + 1)
                nc.vector.tensor_copy(fab[:, e // 2, 2 * (e % 2):2 * (e % 2) + 2, :].rearrange("p a b -> p (a b)"),
                                      bank[2 + e % 4][:, :]).then_inc(fab_ev, 1)
            for m in range(FG):
                dve.wait_ge(fy_h, m + 1)
                nc.vector.tensor_sub(fy_lo[:, m, :], bank[6 + m % 2][:, :], fy_hi[:, m, :].bitcast(F32)).then_inc(fy_l, 1)
            for m in range(H):
                dve.wait_ge(dnh, m + 1)
                nc.vector.tensor_sub(dn_lo[:, m, :], dn[:, m, :], dn_hi[:, m, :].bitcast(F32)).then_inc(dnl, 1)
            dve.wait_ge(four_ev, KB)
            with dve.Fori(0, 2) as i:
                for m in range(4):
                    dve.wait_ge(sig, i * 8 + (2 * m + 1))
                    nc.vector.tensor_tensor(ma[:, 0, :], sg[:, 0, :], fourT[:, bass.ds(i * 4 + m, 1), :].rearrange("p o n -> p (o n)"),
                                            ALU.mult).then_inc(mer_v, 1)
                    dve.wait_ge(sig, i * 8 + (2 * m + 2))
                    dve.wait_ge(mer_mm, i * 12 + (3 * m + 3))
                    nc.vector.tensor_tensor(ma[:, 1, :], sg[:, 1, :], bank[3 * (m % 2) + 2][:, :],
                                            ALU.mult).then_inc(mer_v, 1)
                    dve.wait_ge(mer_v, i * 12 + (3 * m + 2))
                    nc.vector.tensor_tensor(ma[:, 2, :], ma[:, 0, :], ma[:, 1, :], ALU.add).then_inc(mer_v, 1)
                    dve.wait_ge(mgh, i * 4 + (m + 1))
                    nc.vector.tensor_tensor(mg_lo[:, bass.ds(i * 4 + m, 1), :], ma[:, 2:3, :],
                                            mg_hi[:, bass.ds(i * 4 + m, 1), :].bitcast(F32), ALU.subtract).then_inc(mgl, 1)

            def norm(dst, src, n_norm, after_, n_after, gains):
                done = NCH + LAT * (n_norm - 1)
                for t in range(LAT):
                    dve.wait_ge(after_, n_after(t))
                    for i in range(2):
                        nc.vector.bn_stats(stats[:, t, i, :], src[:, t, i * 512:(i + 1) * 512]).then_inc(ln_stat, 1)
                for t in range(LAT):
                    dve.wait_ge(ln_stat, 2 * (done + t) + 2)
                    nc.vector.bn_aggr(mv[:, t, :], stats[:, t, :, :]).then_inc(ln_agg, 1)
                dve.wait_ge(ln_agg, done + LAT)
                nc.vector.tensor_scalar(vare[:, 0:LAT], mv[:, 0:LAT, 1], LN_EPS, None, ALU.add).then_inc(ln_var, 1)
                dve.wait_ge(ln_rstd, n_norm + 1)
                for t in range(LAT):
                    nc.vector.tensor_scalar(dst[:, t, :], src[:, t, :], mv[:, t, 0:1], rstd[:, t:t + 1],
                                            ALU.subtract, ALU.mult).then_inc(ln_out, 1)
                if gains is None:
                    return
                n_gain = LAT * (n_norm // 2)
                for t in range(LAT):
                    dve.wait_ge(ln_out, done + t + 1)
                    nc.vector.tensor_tensor(dst[:, t, :], dst[:, t, :], gains[:, 0, :], ALU.mult).then_inc(ln_gain, 1)
                for t in range(LAT):
                    dve.wait_ge(ln_gain, n_gain + t + 1)
                    nc.vector.tensor_tensor(dst[:, t, :], dst[:, t, :], gains[:, 1, :], ALU.add).then_inc(ln_bias, 1)

            dve.wait_ge(ld_res, 16)
            for t in range(LAT):
                dve.wait_ge(ytr, t + 1)
                for i in range(2):
                    c = slice(i * 512, (i + 1) * 512)
                    nc.vector.scalar_tensor_tensor(x1[:, t, c], x1[:, t, c], ALPHA, bank[2 + 2 * (t % 2) + i][:, :],
                                                   ALU.mult, ALU.add).then_inc(x1_sum, 1)
            dve.wait_ge(ld_gb, 32)
            norm(x1, x1, 1, x1_sum, lambda t: 2 * t + 2, gb)
            norm(xn, x1, 2, ln_bias, lambda t: t + 1, None)
            for k in range(KB):
                dve.wait_ge(h2_hi, k + 1)
                nc.vector.tensor_sub(lat_lo[:, k, :], h2[:, k % 2, :], lat_hi[:, k, :].bitcast(F32)).then_inc(h2_lo, 1)

            def turn(count):
                nc.vector.tensor_copy(mark[:, :], ones[:, 0:1]).then_inc(count, 1)

            def top16(src, cut, vals, ids, n, wait, count):
                turn(count)
                for i in range(n):
                    nc.vector.max(vals[i][:, 0:8], src[i]).then_inc(count, 1)
                wait(n + 1)
                turn(count)
                for i in range(n):
                    nc.vector.max_index(ids[i][:, 0:8], vals[i][:, 0:8], src[i]).then_inc(count, 1)
                    nc.vector.match_replace(cut[i], vals[i][:, 0:8], src[i], -3.0e38).then_inc(count, 1)
                wait(3 * n + 2)
                turn(count)
                for i in range(n):
                    nc.vector.max(vals[i][:, 8:16], cut[i]).then_inc(count, 1)
                wait(4 * n + 3)
                turn(count)
                for i in range(n):
                    nc.vector.max_index(ids[i][:, 8:16], vals[i][:, 8:16], cut[i]).then_inc(count, 1)

            with dve.Fori(0, 2 * PH // 4) as it:
                for j in range(4):
                    dve.wait_ge(s_ev, it * 4 + (j + 1))
                    dve.wait_ge(tk_out, it * 8 + 2 * j)
                    top16([sc[:, j % 2, b, :] for b in range(LAT)], [sc2[:, b, :] for b in range(LAT)],
                          [t16[:, j, b, :] for b in range(LAT)], [i16[:, j, b, :] for b in range(LAT)], LAT,
                          lambda n: dve.wait_ge(tk, it * (4 * TK_N) + (TK_N * j + n)), tk)
                    dve.wait_ge(tk, it * (4 * TK_N) + (TK_N * j + TK_N))
                    o = bass.ds(it * 4 + j, 1)
                    nc.vector.tensor_copy(topv[:, o, :, :], t16[:, j:j + 1, :, :]).then_inc(tk_out, 1)
                    nc.vector.tensor_copy(topi[:, o, :, :], i16[:, j:j + 1, :, :]).then_inc(tk_out, 1)

            dve.wait_ge(tk_out, 4 * PH)
            with dve.Fori(0, LAT) as b:
                made = [0]

                def step(ins):
                    made[0] += 1
                    ins.then_inc(cd, 1)

                def synced():
                    dve.wait_ge(cd, b * CD_N + made[0])

                def side(t, s_):
                    v = t[:, :, bass.ds(b, 1), :].rearrange("p (h s) o k -> p s h (o k)", s=2)
                    return v[:, s_]

                dve.wait_ge(e_tr, b)
                step(nc.vector.tensor_tensor(cand[:, :, :].rearrange("p h (a c) -> p h a c", a=TOPK),
                                             bc(side(topv, 0), TOPK),
                                             side(topv, 1).unsqueeze(2).to_broadcast([P, PH, TOPK, TOPK]), ALU.add))
                synced()
                base = made[0]
                top16([cand[:, h, :] for h in range(PH)], [cand2[:, h, :] for h in range(PH)],
                      [bs[:, h, :] for h in range(PH)], [bj[:, h, :] for h in range(PH)], PH,
                      lambda n: dve.wait_ge(cd, b * CD_N + (base + n)), cd)
                made[0] += 5 * PH + 4
                synced()
                step(nc.vector.tensor_scalar(bja[:, :, :], bj[:, :, :], 4, None, ALU.logical_shift_right))
                step(nc.vector.tensor_scalar(bjc[:, :, :], bj[:, :, :], 15, None, ALU.bitwise_and))
                step(nc.vector.tensor_tensor(bf[4][:, :, :], bs[:, :, :], bc(bs[:, :, 0], TOPK), ALU.subtract))
                assert made[0] == CD_EXP
                synced()
                step(nc.vector.tensor_copy(bf[0][:, :, :], bja[:, :, :]))
                step(nc.vector.tensor_copy(bf[1][:, :, :], bjc[:, :, :]))
                synced()
                for s_ in range(2):
                    io = iota[:, 0:TOPK].unsqueeze(1).to_broadcast([P, PH * TOPK, TOPK])
                    step(nc.vector.tensor_tensor(hot[s_][:, :, :, :].rearrange("p h k a -> p (h k) a"),
                                                 bc(bf[s_][:, :, :].rearrange("p h k -> p (h k)"), TOPK), io, ALU.is_equal))
                for s_ in range(2):
                    synced()
                    step(nc.vector.tensor_tensor(pick[:, :, :, :], hot[s_][:, :, :, :],
                                                 side(topi, s_).unsqueeze(2).to_broadcast([P, PH, TOPK, TOPK]), ALU.mult))
                    synced()
                    nc.vector.tensor_reduce(eidx[:, s_, :].rearrange("p (h k) -> p h k", h=PH), pick[:, :, :, :],
                                            AX.X, ALU.add).then_inc(cd_out, 1)
                    dve.wait_ge(cd_out, b * 3 + (s_ + 1))
                dve.wait_ge(cd_exp, b + 1)
                step(nc.vector.tensor_reduce(bf[6][:, :, 0], bf[5][:, :, :], AX.X, ALU.add))
                synced()
                step(nc.vector.reciprocal(bf[7][:, :, 0], bf[6][:, :, 0]))
                synced()
                nc.vector.tensor_tensor(eidx[:, 2, :].rearrange("p (h k) -> p h k", h=PH), bf[5][:, :, :],
                                        bc(bf[7][:, :, 0], TOPK), ALU.mult).then_inc(cd_out, 1)
                assert made[0] == CD_N

            dve.wait_ge(e_ev, LAT)
            with dve.Fori(0, SEQ // 8) as t:
                for z in range(2):
                    dve.wait_ge(g_mm, t * 2)
                    for w in range(4):
                        col = bass.ds(t * 8 + (4 * z + w), 1)
                        first_ = oh[:, z, w, 0, :]
                        nc.vector.tensor_scalar(first_, iota, eidT[:, 0, col], None, ALU.is_equal).then_inc(oh_done, 1)
                        nc.vector.tensor_scalar(oh[:, z, w, 1, :], iota, eidT[:, 1, col], eidT[:, 2, col],
                                                ALU.is_equal, ALU.mult).then_inc(oh_done, 1)

            for j in range(2):
                dve.wait_ge(gs_st[j], SEQ // GTOK // 2 * 16)
            nc.vector.memset(acc[:, :, :].rearrange("p a b -> p (a b)"), 0.0).then_inc(acc_zero, 1)
            dve.wait_ge(acc_zero, 1)

            def dve_c(i, loc, quads):
                slot = loc // 4 % 2
                dve.wait_ge(gelu, i + (loc + 1))
                dve.wait_ge(gq_full[slot], quads)
                if loc >= 2:
                    dve.wait_ge(cl, i + (loc - 1))
                nc.vector.tensor_tensor(cf[:, loc % 2, :].rearrange("p (g t) -> p g t", t=GTOK),
                                        gl[:, loc % 2, :].rearrange("p (g t) -> p g t", t=GTOK),
                                        gq[:, slot, :, loc % 4, :], ALU.mult).then_inc(cf_done, 1)

            def dve_cl(i, loc):
                dve.wait_ge(ch, i + (loc + 1))
                nc.vector.tensor_sub(c_lo[:, loc % 4, :], cf[:, loc % 2, :],
                                     c_hi[:, loc % 4, :].bitcast(F32)).then_inc(cl, 1)

            def dve_acc(i, r_, k):
                dve.wait_ge(v_mm, i * 4 + (8 * r_ + k + 1))
                nc.vector.tensor_tensor(acc[:, k, :], acc[:, k, :], bank[2 + k % 6][:, :], ALU.add).then_inc(acc_done, 1)

            def dve_pairs(q, i, n_pair, last):
                for r_ in range(n_pair):
                    end = last and r_ == n_pair - 1
                    if not end:
                        dve_c(i, 2 * r_ + 2, q * 16 + ((2 * r_ + 2) // 8 + 1) * 16)
                    dve_acc(i, r_, 0)
                    if not end:
                        dve_cl(i, 2 * r_ + 2)
                    for k in range(1, KB):
                        dve_acc(i, r_, k)
                    if not end:
                        dve_c(i, 2 * r_ + 3, q * 16 + ((2 * r_ + 3) // 8 + 1) * 16)
                        dve_cl(i, 2 * r_ + 3)

            for j in range(2):
                dve_c(0, j, 16)
                dve_cl(0, j)
            with dve.Fori(0, N_IT) as q:
                dve_pairs(q, q * 8, 4, False)
            dve_pairs(N_IT, N_IT * 8, 4, True)
            for t in range(LAT):
                dve.wait_ge(fin_tr, t + 1)
                for i in range(2):
                    c = slice(i * 512, (i + 1) * 512)
                    nc.vector.scalar_tensor_tensor(xo[:, t, c], x1[:, t, c], ALPHA, bank[2 * (t % 2) + i][:, :],
                                                   ALU.mult, ALU.add).then_inc(xo_sum, 1)
            dve.wait_ge(ld_gb, 64)
            norm(xo, xo, 3, xo_sum, lambda t: 2 * t + 2, gb2)

        @block.tensor
        def _(pe):
            mm, transpose = nc.tensor.matmul, nc.tensor.transpose

            def ada_tile(slot, out):
                for k in range(KB):
                    last = mm(out, ada[:, slot, k * P:(k + 1) * P], cond_s[:, k, :], start=k == 0, stop=k == KB - 1)
                last.then_inc(ada_mm, 1)

            pe.wait_ge(cond_done, 1)
            with pe.Fori(0, ADA_FIRST // 2) as i:
                for j in range(2):
                    pe.wait_ge(ada_full[j], i * 16 + 16)
                    ada_tile(j, bank[7][:, bass.ds(i * 4 + 2 * j, 2)])
            pe.wait_ge(ld_cst, 16)
            pe.wait_ge(ln_out, NCH)
            for k in range(KB):
                if k >= 2:
                    pe.wait_ge(hin_mod, 2 * (k - 1))
                for t in range(NCH):
                    dst = bank[2 + k % 2][:, t * P:(t + 1) * P] if t < CT else bank[k % 2][:, (t - CT) * P:(t - CT + 1) * P]
                    last = transpose(dst, xin[:, t, k * P:(k + 1) * P], ident)
                last.then_inc(hin_tr, 1)
            pe.wait_ge(ab_split, 2)
            pe.wait_ge(hin_lo, 2 * KB)
            for t in range(NCH):
                xh, xl, c = (ctx_hi, ctx_lo, t) if t < CT else (lat_hi, lat_lo, t - CT)
                for k in range(KB):
                    last = mm3(bank[4][:, t * 32:(t + 1) * 32], xh[:, k, c * P:(c + 1) * P], xl[:, k, c * P:(c + 1) * P],
                               ab_hi[:, k, :], ab_lo[:, k, :], k == 0, k == KB - 1)
            last.then_inc(ab_mm, 1)
            pe.wait_ge(gate_done, 2)
            for d in range(NDIR):
                v = gall[:, :].rearrange("p (a d c) -> p d a c", d=NDIR, c=2)[:, d]
                o = bank[5][:, 0:H * NU].rearrange("p (a d c) -> p d a c", d=NDIR, c=2)[:, d]
                mm(o, u_dir(d), v, start=True, stop=True).then_inc(cum_mm, 1)
            mm(bank[5][:, H * NU:2 * H * NU], ones, gall[:, :], start=True, stop=True).then_inc(cum_mm, 1)
            pe.wait_ge(gate_done, 5)

            with pe.Fori(0, H) as h:
                o = 0
                for j in range(4):
                    pe.wait_ge(split_done, h * 4 + (j + 1))
                    for lat in ((True, False) if j < 2 else (True,)):
                        if o == 1:
                            pe.wait_ge(z_done, h)
                        else:
                            pe.wait_ge(conv, h * 5 + max(o - 1, 0))
                        xh, xl, n = (lat_hi, lat_lo, SEQ) if lat else (ctx_hi, ctx_lo, CTX)
                        for k in range(KB):
                            last = mm3(bank[o % 2][:, 0:n], *w_block(j, k), xh[:, k, :], xl[:, k, :],
                                       k == 0, k == KB - 1)
                        last.then_inc(proj, 1)
                        o += 1
                pe.wait_ge(state, h * 10)
                for j in range(4):
                    pe.wait_ge(ada_full[j % 2], h * 32 + (8 + j // 2 + 1) * 16)
                    ada_tile(j % 2, bank[7][:, 256 + 2 * j:258 + 2 * j])
                pe.wait_ge(dn_done, h)
                for src, n, b0, count in ((kT, NCH, 2, 2), (qT, LAT, 4, 5), (vT, NCH, 5, 4)):
                    pe.wait_ge(silu, h * 5 + count)
                    for c in range(n):
                        last = transpose(bank[b0 + c // 4][:, (c % 4) * P:(c % 4 + 1) * P], src[:, c * P:(c + 1) * P], ident)
                    last.then_inc(tr, 1)
                pe.wait_ge(sq_done, h * 2 + 2)
                pe.wait_ge(mods_done, h + 3)
                for c in range(NCH + LAT):
                    last = mm(bank[7][:, c:c + 1], sqv[:, c * P:(c + 1) * P], ones[:, 0:1], start=True, stop=True)
                last.then_inc(ssq, 1)
                for src, n, b0, count in ((Kn, NCH, 2, 2), (Qn, LAT, 4, 3)):
                    pe.wait_ge(kn, h * 3 + count)
                    for c in range(n):
                        last = transpose(bank[b0 + c // 4][:, (c % 4) * P:(c % 4 + 1) * P], src[:, c, :], ident)
                    last.then_inc(trb, 1)
                pe.wait_ge(gst_done, h + 1)
                pe.wait_ge(vev, h * 2 + 2)
                for g in range(NG):
                    for q in range(4):
                        last = mm(bank[5 + g][:, q * P:(q + 1) * P], gst[:, 4 * g + q, :], u_dir(q // 2), start=True, stop=True)
                    last.then_inc(gbc, 1)
                pe.wait_ge(knt, h * 3 + 3)
                for c in range(NCH):
                    kc = knT[:, c * P:(c + 1) * P]
                    last = mm(bank[2 + c // 4][:, (c % 4) * P:(c % 4 + 1) * P], kc, kc, start=True, stop=True)
                last.then_inc(kk, 1)
                for c in range(LAT):
                    last = mm(bank[4][:, c * P:(c + 1) * P], knT[:, (c + CT) * P:(c + CT + 1) * P],
                              qnT[:, c * P:(c + 1) * P], start=True, stop=True)
                last.then_inc(kk, 1)
                pe.wait_ge(lt, h * 12 + 12)
                pe.wait_ge(att_done, h * 2 + 2)
                for g in range(NG):
                    for q in range(4):
                        last = transpose(bank[2 + g][:, q * P:(q + 1) * P], Lt[:, 4 * g + q, :], ident)
                    last.then_inc(n1, 1)
                for g in range(NG):
                    pe.wait_ge(nn, h * 21 + (g + 1))
                    for q in range(4):
                        last = transpose(bank[5 + g][:, q * P:(q + 1) * P], eN[:, 4 * g + q, :], ident)
                    last.then_inc(xy, 1)

                def level(done, last_level):
                    for g in range(NG):
                        pe.wait_ge(y_done, done[1] + (g + 1))
                        for q in range(4):
                            last = mm(bank[2 + g][:, q * P:(q + 1) * P], Lt[:, 4 * g + q, :], dY[:, 4 * g + q, :],
                                      start=True, stop=True)
                        last.then_inc(n1, 1)
                    for g in range(NG):
                        pe.wait_ge(x_done, done[0] + (g - 2))
                        pe.wait_ge(nn, done[0] + (g + 1))
                        for q in range(4):
                            u, c = 4 * g + q, slice(q * P, (q + 1) * P)
                            if not last_level:
                                mm(bank[2 + g][:, c], gX[:, u, :], eN[:, u, :], start=True, stop=True)
                            last = mm(bank[5 + g][:, c], eN[:, u, :], gX[:, u, :], start=True, stop=True)
                        last.then_inc(xy, 1)

                with pe.Fori(1, LEVELS - 1) as lv:
                    level((h * 21 + lv * 3, h * 18 + lv * 3 - 3), False)
                level((h * 21 + (LEVELS - 1) * 3, h * 18 + (LEVELS - 2) * 3), True)
                pe.wait_ge(x_done, h * 21 + 21)
                pe.wait_ge(kts, h * 4 + 4)
                pe.wait_ge(kd_done, h * 2 + 2)
                first = True
                for s in range(NCH):
                    lat = s >= CT
                    for d in range(NDIR):
                        if not s:
                            continue
                        c = walk(d)[s]
                        pe.wait_ge(state, h * 10 + (2 * (s - 1) + d + 1))
                        mm(bank[3 + d][:, 0:P], kTs[:, unit(d, c), :], St[:, d, (s - 1) % 2, :], start=True,
                           stop=True).then_inc(ks, 1)
                        if lat:
                            mm(bank[2][:, (c - CT) * P:(c - CT + 1) * P], St[:, d, (s - 1) % 2, :],
                               qTs[:, (c - CT) // 2, d, (c % 2) * P:(c % 2 + 1) * P], start=first, stop=False,
                               skip_group_check=True)
                            first = False
                    for d in range(NDIR):
                        c = walk(d)[s]
                        if s:
                            pe.wait_ge(res, h * 10 + (2 * (s - 1) + d + 1))
                        rhs = Rd[:, d, :] if s else Vt[:, c, :]
                        mm(bank[5 + d][:, 0:P], gX[:, unit(d, c), :], rhs, start=True, stop=True).then_inc(solve, 1)
                    for d in range(NDIR):
                        c = walk(d)[s]
                        pe.wait_ge(vn, h * 12 + (2 * s + d + 1))
                        if s < NCH - 1:
                            mm(bank[3 + d][:, 0:P], Kd[:, unit(d, c), :], Vn[:, d, :], start=True,
                               stop=True).then_inc(kdv, 1)
                        if lat:
                            end = s == NCH - 1 and d == 1
                            last = mm(bank[2][:, (c - CT) * P:(c - CT + 1) * P], Vn[:, d, :],
                                      att[:, (c - CT) // 2, d, (c % 2) * P:(c % 2 + 1) * P], start=False, stop=end,
                                      skip_group_check=True)
                            if end:
                                last.then_inc(o_done, 1)
                pe.wait_ge(sqo, h + 1)
                for c in range(LAT):
                    last = mm(bank[3][:, c:c + 1], sqv[:, c * P:(c + 1) * P], ones[:, 0:1], start=True, stop=True)
                last.then_inc(ssqo, 1)
                pe.wait_ge(rst_done, h + 1)
                for c in range(LAT):
                    last = mm(bank[4][:, c * P:(c + 1) * P], rst[:, c, :], ident, start=True, stop=True)
                last.then_inc(rbc_mm, 1)

            for m in range(FG):
                pe.wait_ge(split_done, T_F + m + 1)
                if m == 0:
                    pe.wait_ge(dn_done, H)
                if m >= 2:
                    pe.wait_ge(f_ev, m - 1)
                for k in range(KB):
                    last = mm3(bank[m % 2][:, :], *w_block(m, k), lat_hi[:, k, :], lat_lo[:, k, :], k == 0, k == KB - 1)
                last.then_inc(f_mm, 1)
            dft_c = cst[:, C_DFT:C_DFT + 2 * P]
            for e in range(2 * FG):
                pe.wait_ge(f_ev, e // 2 + 1)
                if e >= 4:
                    pe.wait_ge(fab_ev, e - 3)
                for b in range(2):
                    t = 2 * (e % 2) + b
                    last = mm(bank[2 + e % 4][:, b * 256:(b + 1) * 256], fT[:, e // 2, t * P:(t + 1) * P], dft_c,
                              start=True, stop=True)
                last.then_inc(fab_mm, 1)
            pe.wait_ge(ld_dft, 16)
            for m in range(FG):
                pe.wait_ge(fab_ev, 2 * m + 2)
                if m >= 2:
                    pe.wait_ge(fy_l, m - 1)
                for e in range(2):
                    for t in range(LAT):
                        last = mm(bank[6 + m % 2][:, :], fab[:, m, t, e * P:(e + 1) * P], dft[:, e, t, :],
                                  start=e + t == 0, stop=e == 1 and t == LAT - 1)
                last.then_inc(fy_mm, 1)
            pe.wait_ge(fy_l, FG)
            for m in range(KB):
                if m % 2 == 0:
                    pe.wait_ge(split_done, T_FOUR + m // 2 + 1)
                if m >= 2:
                    pe.wait_ge(four_ev, m - 1)
                for k in range(FG):
                    last = mm3(bank[m % 2][:, :], *w_block(m // 2, (m % 2) * FG + k), fy_hi[:, k, :], fy_lo[:, k, :],
                               k == 0, k == FG - 1)
                last.then_inc(four_mm, 1)
            pe.wait_ge(dnl, H)
            pe.wait_ge(four_ev, KB)
            with pe.Fori(0, 2) as i:
                for m in range(4):
                    for t in range(3):
                        n = 3 * m + t
                        pe.wait_ge(split_done, i * 12 + (T_MERGE + n + 1))
                        if m >= 2:
                            pe.wait_ge(mer_v, i * 12 + 3 * (m - 1))
                        xh, xl = (lat_hi, lat_lo) if t < 2 else (dn_hi, dn_lo)
                        for k in range(KB):
                            last = mm3(bank[3 * (m % 2) + t][:, :], *w_block(n % RING, k), xh[:, k, :], xl[:, k, :],
                                       k == 0, k == KB - 1)
                        last.then_inc(mer_mm, 1)
                pe.wait_ge(mer_v, i * 12 + 12)
            pe.wait_ge(mgl, KB)
            for m in range(KB):
                pe.wait_ge(split_done, T_OUT + m + 1)
                if m >= 2:
                    pe.wait_ge(yt_done, m - 1)
                for k in range(KB):
                    last = mm3(bank[m % 2][:, :], *w_block(m % RING, k), mg_hi[:, k, :], mg_lo[:, k, :],
                               k == 0, k == KB - 1)
                last.then_inc(out_mm, 1)
            pe.wait_ge(yt_done, KB)
            for t in range(LAT):
                if t >= 2:
                    pe.wait_ge(x1_sum, 2 * (t - 1))
                for k in range(KB):
                    last = transpose(bank[2 + 2 * (t % 2) + k // 4][:, (k % 4) * P:(k % 4 + 1) * P],
                                     yT[:, k, t * P:(t + 1) * P], ident)
                last.then_inc(ytr, 1)
            pe.wait_ge(ln_out, NCH + 2 * LAT)
            for k in range(KB):
                if k >= 2:
                    pe.wait_ge(h2_mod, k - 1)
                for t in range(LAT):
                    last = transpose(bank[k % 2][:, t * P:(t + 1) * P], xn[:, t, k * P:(k + 1) * P], ident)
                last.then_inc(h2_tr, 1)
            pe.wait_ge(h2_lo, KB)
            pe.wait_ge(ld_sk, 16)
            with pe.Fori(0, 2 * PH // 4) as i:
                for j in range(4):
                    pe.wait_ge(split_done, i * 4 + (T_QUERY + j + 1))
                    pe.wait_ge(q_ev, i * 4 + max(j - 1, 0))
                    for k in range(KB):
                        last = mm3(bank[j % 2][:, :], *w_block(j, k), lat_hi[:, k, :], lat_lo[:, k, :],
                                   k == 0, k == KB - 1)
                    last.then_inc(q_mm, 1)
                    pe.wait_ge(q_ev, i * 4 + (j + 1))
                    pe.wait_ge(s_ev, i * 4 + max(j - 1, 0))
                    for b in range(LAT):
                        last = mm(bank[2 + j % 2][:, b * P:(b + 1) * P], qq[:, j, b * P:(b + 1) * P],
                                  sk[:, bass.ds(i * 4 + j, 1), :].rearrange("p o n -> p (o n)"), start=True, stop=True)
                    last.then_inc(s_mm, 1)
            with pe.Fori(0, LAT) as b:
                pe.wait_ge(cd_out, b * 3 + 3)
                pe.wait_ge(e_ev, b)
                for r_ in range(3):
                    last = transpose(bank[4][:, r_ * P:(r_ + 1) * P], eidx[:, r_, :], ident)
                last.then_inc(e_tr, 1)
            with pe.Fori(0, SEQ // 8) as t:
                for z in range(2):
                    pe.wait_ge(oh_done, t * 16 + (8 * z + 8))
                    if z == 0:
                        pe.wait_ge(g_ev, t * 2)
                    for w in range(4):
                        last = mm(bank[z][:, w * P:(w + 1) * P], oh[:, z, w, 1, :], oh[:, z, w, 0, :], start=True, stop=True)
                    last.then_inc(g_mm, 1)

            def pe_a(i, n, loc, slot):
                pe.wait_ge(split_done, n + 1)
                if loc >= 2:
                    pe.wait_ge(gelu, i + (loc - 1))
                for k in range(KB):
                    last = mm3(bank[loc % 2][:, :], *w_block(slot, k), lat_hi[:, k, :], lat_lo[:, k, :],
                               k == 0, k == KB - 1)
                last.then_inc(a_mm, 1)

            def pe_v(i, n, r_, slots):
                pe.wait_ge(split_done, n + 2)
                pe.wait_ge(cl, i + (2 * r_ + 2))
                for k in range(KB):
                    if r_ or k >= 6:
                        pe.wait_ge(acc_done, i * 4 + (8 * r_ + k - 5))
                    for y in range(2):
                        c_ = (2 * r_ + y) % 4
                        last = mm3(bank[2 + k % 6][:, :], *w_block(slots[y], k), c_hi[:, c_, :], c_lo[:, c_, :],
                                   y == 0, y == 1)
                    last.then_inc(v_mm, 1)

            def pe_pairs(q, i, n, n_pair, last_):
                for r_ in range(n_pair):
                    end = last_ and r_ == n_pair - 1
                    if end:
                        pe_v(i, n + 4 * r_, r_, (2, 3))
                    else:
                        pe_a(i, n + 4 * r_, 2 * r_ + 2, 2)
                        pe_v(i, n + (4 * r_ + 1), r_, (3, 0))
                        pe_a(i, n + (4 * r_ + 3), 2 * r_ + 3, 1)

            for j in range(2):
                pe.wait_ge(g_ev, SEQ // 4)
                pe_a(0, T_PEER + j, j, j)
            with pe.Fori(0, N_IT) as q:
                pe_pairs(q, q * 8, q * 16 + (T_PEER + 2), 4, False)
                pe.wait_ge(acc_done, q * 32 + 32)
            pe_pairs(N_IT, N_IT * 8, N_IT * 16 + T_PEER + 2, 4, True)
            pe.wait_ge(fin, KB)
            for t in range(LAT):
                if t >= 2:
                    pe.wait_ge(xo_sum, 2 * (t - 1))
                for k in range(KB):
                    last = transpose(bank[2 * (t % 2) + k // 4][:, (k % 4) * P:(k % 4 + 1) * P],
                                     acc[:, k, t * P:(t + 1) * P], ident)
                last.then_inc(fin_tr, 1)


def lay_out(x, c, ctx, c_ctx, w_ada, b_ada, w_in, conv_w, a_log, dt_bias, dn_norm_w, w_four, w_dn,
            w_out, ln_g, ln_b, peer_w_query, peer_sub_keys, peer_u, peer_v):
    f = np.float32

    def tiles(w):
        k, n = w.shape
        return w.reshape(k // P, P, n // P, P).transpose(2, 1, 0, 3)

    def flat(t):
        return np.ascontiguousarray(t, dtype=f).reshape(-1, P, KB * P)

    w_in = np.asarray(w_in[0])
    n_ab = 2 * NDIR * H
    wide = tiles(w_in[:, n_ab:])
    k_, v_, q_, z_ = (wide[i * H:(i + 1) * H] for i in range(4))
    f_ = wide[4 * H:4 * H + FG]
    g_ = wide[4 * H + FG:]
    four = tiles(np.asarray(w_four[0])).reshape(FG, 2, P, FG, P).transpose(0, 2, 1, 3, 4)
    dn_t = tiles(np.asarray(w_dn[0]))
    order = [flat(np.stack([k_, v_, q_, z_], 1)), flat(f_), flat(four),
             flat(np.stack([g_[:KB], g_[KB:], dn_t], 1)), flat(tiles(np.asarray(w_out[0]))),
             flat(tiles(np.asarray(peer_w_query[0])))]
    u = np.asarray(peer_u[0]).reshape(PK, PK, KB, P).transpose(0, 3, 2, 1).reshape(PK, P, KB * P)
    v = np.asarray(peer_v[0]).reshape(PK, P, KB * P)
    seq = [u[0], u[1]]
    for pair in range(PK // 2):
        seq += [u[(2 * pair + 2) % PK], v[2 * pair], v[2 * pair + 1], u[(2 * pair + 3) % PK]]
    order.append(np.stack(seq[:2 * PK - 2] + [v[PK - 2], v[PK - 1]]).astype(f))
    cst, dft = constants()
    two = np.stack([np.asarray(c)[0], np.asarray(c_ctx)], -1)
    return {
        "w": np.concatenate(order),
        "w_ada": flat(tiles(np.asarray(w_ada[0]))),
        "b_ada": np.ascontiguousarray(np.asarray(b_ada[0]).reshape(ADA_ALL, P).T),
        "cond": np.ascontiguousarray(two.reshape(KB, P, 2).transpose(1, 0, 2)),
        "x": np.ascontiguousarray(x[0]),
        "ctx": np.ascontiguousarray(ctx[0]),
        "cst": cst,
        "dft": dft,
        "ab_w": np.ascontiguousarray(w_in[:, :n_ab].reshape(KB, P, n_ab).transpose(1, 0, 2)),
        "dtb": np.ascontiguousarray(np.asarray(dt_bias[0]).reshape(-1)),
        "alog": np.ascontiguousarray(np.asarray(a_log[0]).reshape(-1)),
        "cw": np.ascontiguousarray(np.asarray(conv_w[0]).reshape(TAPS, 3 * H, P).transpose(2, 0, 1)),
        "nrm_w": np.ascontiguousarray(np.asarray(dn_norm_w[0]).reshape(P, 1)),
        "ln": np.ascontiguousarray(np.concatenate([np.asarray(ln_g[0]), np.asarray(ln_b[0])]).reshape(4, D)),
        "sub_keys": np.ascontiguousarray(np.asarray(peer_sub_keys[0]).reshape(2 * PH, PK, P).transpose(2, 0, 1)),
    }


def kernel(**inputs):
    import numpy as _np
    import concourse.bacc as _bacc
    from concourse.bass_utils import run_bass_kernel_spmd as _run

    nc = _bacc.Bacc("TRN2", target_bir_lowering=False, num_devices=1)
    arrays = lay_out(**inputs)
    aps = {n: nc.dram_tensor(n, a.shape, mybir.dt.from_np(a.dtype), kind="ExternalInput").ap() for n, a in arrays.items()}
    aps["out"] = nc.dram_tensor("out", (SEQ, D), F32, kind="ExternalOutput").ap()
    layer_kernel(nc, aps)
    r = _run(nc, [arrays], core_ids=[0])
    return _np.asarray(r.results[0]["out"]).reshape(1, SEQ, D)
```

```python
import math
from contextlib import ExitStack

import numpy as np

import concourse.bass as bass
from concourse import mybir

F32 = mybir.dt.float32
F32R = mybir.dt.float32r
U32 = mybir.dt.uint32
ACT = mybir.ActivationFunctionType
ALU = mybir.AluOpType
AX = mybir.AxisListType

P = 128
D = 1024
KB = D // P
SEQ, CTX, GRID_W = 512, 256, 64
LAT = SEQ // P
CT = CTX // P
NCH = CT + LAT
H = 8
NDIR = 2
NU = NCH * NDIR
NG = NU // 4
TAPS = 5
LEVELS = 7
FG = 4
PH, PK, TOPK = 8, 128, 16
ALPHA = 2.0 ** 0.25
LN_EPS = 1e-6
RMS_EPS = 1e-6
L2_EPS = 1e-6
FAR = -1.0e30
GTOK = 64
TK_N = 24
CD_N, CD_EXP = 56, 48
N_IT = PK // 8 - 1

T_HEAD = 0
T_F = T_HEAD + 4 * H
T_FOUR = T_F + FG
T_MERGE = T_FOUR + 4
T_OUT = T_MERGE + 3 * KB
T_QUERY = T_OUT + KB
T_U = T_QUERY + 4 * PH
T_V = T_U + PK - 2 * PH
T_ALL = T_V + PK
U_CD = 8
X_CD = 2 * PH
X_G = X_CD + LAT * U_CD
X_END = X_G + SEQ // 8
RING = 4
RAW = 2
ADA_FIRST = 2 * KB
ADA_ALL = 6 * KB

C_ID = 0
C_U = C_ID + P
C_NEG = C_U + 2 * P
C_LVL = C_NEG + 2 * P
C_ONE = C_LVL + LEVELS * 2 * P
C_IOTA = C_ONE + P
C_DFT = C_IOTA + P
C_ALL = C_DFT + 2 * P


def constants():
    c = np.zeros((P, C_ALL), np.float32)
    r = np.arange(P)
    c[:, C_ID:C_ID + P] = np.eye(P)
    j, i = r[:, None], r[None, :]
    c[:, C_U:C_U + P] = j <= i
    c[:, C_U + P:C_U + 2 * P] = j >= i
    c[:, C_NEG:C_NEG + P] = np.where(j <= i, 0.0, FAR)
    c[:, C_NEG + P:C_NEG + 2 * P] = np.where(j >= i, 0.0, FAR)
    for lv in range(LEVELS):
        s = 1 << lv
        same = (j // (2 * s)) == (i // (2 * s))
        low = same & ((j // s) % 2 == 1) & ((i // s) % 2 == 0)
        c[:, C_LVL + (2 * lv) * P:C_LVL + (2 * lv + 1) * P] = -1.0 * low
        c[:, C_LVL + (2 * lv + 1) * P:C_LVL + (2 * lv + 2) * P] = -1.0 * low.T
    c[:, C_ONE:C_ONE + P] = 1.0
    c[:, C_IOTA:C_IOTA + P] = r[None, :]
    a = 2 * np.pi * ((j * i) % P) / P
    c[:, C_DFT:C_DFT + P] = np.cos(a) / math.sqrt(P)
    c[:, C_DFT + P:] = np.sin(a) / math.sqrt(P)
    t = np.arange(SEQ)
    b = 2 * np.pi * ((t[:, None] * t[None, :]) % SEQ) / SEQ
    dft = np.stack([np.cos(b) / math.sqrt(SEQ), -np.sin(b) / math.sqrt(SEQ)])
    dft = dft.reshape(2, LAT, P, SEQ).transpose(2, 0, 1, 3).astype(np.float32)
    return c, np.ascontiguousarray(dft)


def bc(ap, n):
    shape = [int(s) for s in ap.shape]
    return ap.unsqueeze(len(shape)).to_broadcast([*shape, n])


def rep(ap, n):
    shape = [int(s) for s in ap.shape]
    return ap.unsqueeze(1).to_broadcast([shape[0], n, *shape[1:]])


class Map:

    def __init__(self, nc, at, end):
        self.nc, self.at, self.end = nc, at, end

    def branch(self):
        return Map(self.nc, self.at, self.end)

    def __call__(self, name, shape, dt=F32):
        t = self.nc.alloc_sbuf_tensor_at(name, [P, *shape], dt, offset=self.at)
        self.at += (4 * int(np.prod(shape)) + 31) // 32 * 32
        assert self.at <= self.end, (name, self.at, self.end)
        return t


def layer_kernel(nc, A):
    stack = ExitStack()
    with stack:
        def sem(name):
            return stack.enter_context(nc.semaphore(name))

        def sems(name, n):
            return [sem(f"{name}{i}") for i in range(n)]

        bank = [stack.enter_context(nc.psum_tensor(f"bank{i}", [P, 512], F32)) for i in range(8)]

        buf = Map(nc, (nc.sbuf_base + 31) // 32 * 32, nc.sbuf_usable_end)
        cst = buf("cst", [C_ALL])
        raw = buf("raw", [RAW, KB * P])
        w_hi = buf("w_hi", [RING, KB * P], F32R)
        w_lo = buf("w_lo", [RING, KB * P], F32R)
        lat_hi = buf("lat_hi", [KB, SEQ], F32R)
        lat_lo = buf("lat_lo", [KB, SEQ], F32R)
        mods = buf("mods", [ADA_ALL, 2])
        b_ada = buf("b_ada", [ADA_ALL])
        cond = buf("cond", [KB, 2])
        cond_s = buf("cond_s", [KB, 2])
        stats = buf("stats", [NCH, 2, 6])
        mv = buf("mv", [NCH, 2])
        vare = buf("vare", [NCH])
        rstd = buf("rstd", [NCH])
        nhalf = buf("nhalf", [16])
        mark = buf("mark", [1])
        ident = cst[:, C_ID:C_ID + P]
        ones = cst[:, C_ONE:C_ONE + P]
        iota = cst[:, C_IOTA:C_IOTA + P]

        def u_dir(d):
            return cst[:, C_U + d * P:C_U + (d + 1) * P]

        def neg_dir(d):
            return cst[:, C_NEG + d * P:C_NEG + (d + 1) * P]

        after = buf.branch()
        dn = buf("dn", [H, SEQ])
        fou = buf.branch()
        ctx_hi = buf("ctx_hi", [KB, CTX], F32R)
        ctx_lo = buf("ctx_lo", [KB, CTX], F32R)
        ada = buf("ada", [2, KB * P])
        beta = buf("beta", [H * NU])
        gall = buf("gall", [H * NU])
        gcum = buf("gcum", [H * NU])
        kds = buf("kds", [H * NU])
        egl = buf("egl", [H * NU])
        cw = buf("cw", [TAPS, 3 * H])
        nrm_w = buf("nrm_w", [1])

        inp = buf.branch()
        xin = inp("xin", [NCH, D])
        hm = inp("hm", [2, NCH * P])
        ab_w = inp("ab_w", [KB, 32])
        ab_hi = inp("ab_hi", [KB, 32], F32R)
        ab_lo = inp("ab_lo", [KB, 32], F32R)
        dtb = inp("dtb", [16])
        alog = inp("alog", [16])
        expa = inp("expa", [16])
        sp = [inp(f"sp{i}", [H * NU]) for i in range(18)]
        abT = inp("abT", [NCH * P])
        ada_a = inp("ada_a", [8, KB * P])
        ada_b = dn[:, :, :].rearrange("p (m a) n -> p m (a n)", m=4)

        cv = buf("cv", [2, SEQ])
        kT = buf("kT", [NCH * P])
        vT = buf("vT", [NCH * P])
        qT = buf("qT", [SEQ])
        rr = buf("rr", [2, 16])
        rn = buf("rn", [16])
        ro = buf("ro", [4])
        rno = buf("rno", [4])
        Kn = buf("Kn", [NCH, P])
        Qn = buf("Qn", [LAT, P])
        Vt = buf("Vt", [NCH, P])
        knT = buf("knT", [NCH * P])
        qnT = buf("qnT", [SEQ])
        gX = buf("gX", [NU, P])
        eN = buf("eN", [NU, P])
        dY = buf("dY", [NU, P])
        Lt = buf("Lt", [NU, P])
        att = buf("att", [2, NDIR, 2 * P])
        kTs = buf("kTs", [NU, P])
        qTs = buf("qTs", [2, NDIR, 2 * P])
        Kd = buf("Kd", [NU, P])
        Rd = buf("Rd", [NDIR, P])
        Vn = buf("Vn", [NDIR, P])
        St = buf("St", [NDIR, 2, P])
        gst = gX
        sqv = Lt[:, :, :].rearrange("p a b -> p (a b)")
        rst = kTs[:, 0:LAT, :]
        rbc = kTs[:, LAT:2 * LAT, :].rearrange("p a b -> p (a b)")
        onT = kTs[:, 2 * LAT:3 * LAT, :].rearrange("p a b -> p (a b)")

        fy_hi = ctx_hi[:, :, :].rearrange("p a b -> p (a b)").rearrange("p (a b) -> p a b", a=FG)
        fy_lo = ctx_lo[:, :, :].rearrange("p a b -> p (a b)").rearrange("p (a b) -> p a b", a=FG)
        fou.at += 4 * 2 * KB * CTX
        fourT = fou("fourT", [KB, SEQ])
        mer = fou.branch()
        fT = fou("fT", [FG, SEQ])
        fab = fou("fab", [FG, LAT, 2 * P])
        dft = fou("dft", [2, LAT, SEQ])

        low = after.branch()
        low.at += 4 * H * SEQ
        sg = low("sg", [2, SEQ])
        ma = low("ma", [3, SEQ])
        assert low.at <= mer.at - 4 * KB * SEQ
        dn_hi = mer("dn_hi", [H, SEQ], F32R)
        dn_lo = mer("dn_lo", [H, SEQ], F32R)
        mg_hi = mer("mg_hi", [KB, SEQ], F32R)
        mg_lo = mer("mg_lo", [KB, SEQ], F32R)

        x1 = after("x1", [LAT, D])
        pst = after.branch()
        yT = pst("yT", [KB, SEQ])
        gb = pst("gb", [2, D])
        h2 = pst("h2", [2, SEQ])
        xn = pst("xn", [LAT, D])
        pst_end = pst.at

        eidx = after("eidx", [3, P])
        eidT = after("eidT", [3, SEQ])
        gu = after("gu", [2, SEQ])
        keys = after.branch()
        sk = keys("sk", [2 * PH, P])
        qq = keys("qq", [RING, SEQ])
        sc = keys("sc", [2, LAT, P])
        sc2 = keys("sc2", [LAT, P])
        t16 = keys("t16", [RING, LAT, TOPK])
        i16 = keys("i16", [RING, LAT, TOPK], U32)
        topv = keys("topv", [2 * PH, LAT, TOPK])
        topi = keys("topi", [2 * PH, LAT, TOPK])
        cand = keys("cand", [PH, TOPK * TOPK])
        cand2 = keys("cand2", [PH, TOPK * TOPK])
        bs = keys("bs", [PH, TOPK])
        bj = keys("bj", [PH, TOPK], U32)
        bja = keys("bja", [PH, TOPK], U32)
        bjc = keys("bjc", [PH, TOPK], U32)
        bf = [keys(f"bf{i}", [PH, TOPK]) for i in range(8)]
        hot = [keys(f"hot{i}", [PH, TOPK, TOPK]) for i in range(2)]
        pick = keys("pick", [PH, TOPK, TOPK])
        gates = after.branch()
        oh = gates("oh", [2, 4, 2, P])
        gs = gates("gs", [2, P, GTOK])
        gl = gates("gl", [2, 4, SEQ])

        g_dram = nc.dram_tensor("g_dram", (SEQ // GTOK, P, PK, GTOK), F32, kind="Internal").ap()

        gu_dram = nc.dram_tensor("gu_dram", (PK, P, SEQ), F32, kind="Internal").ap()

        acc = after("acc", [KB, SEQ])
        c_hi = after("c_hi", [4, SEQ], F32R)
        c_lo = after("c_lo", [4, SEQ], F32R)
        cf = after("cf", [2, SEQ])
        gq = after("gq", [2, SEQ // GTOK, 4, GTOK])
        gb2 = after("gb2", [2, D])
        assert after.at <= gates.at - 4 * 8 * SEQ
        xo = after("xo", [LAT, D])

        ld_cst, ld_cond, ld_ab, ld_head = sem("ld_cst"), sem("ld_cond"), sem("ld_ab"), sem("ld_head")
        ld_x = sems("ld_x", NCH)
        raw_full = sems("raw_full", RAW)
        ada_full = sems("ada_full", 2)
        ada_in = sems("ada_in", ADA_FIRST // 4)
        hi_done = sem("hi_done")
        split_done = sem("split_done")
        nhalf_set = sem("nhalf_set")
        cond_done = sem("cond_done")
        ada_mm = sem("ada_mm")
        mods_done = sem("mods_done")
        ln_stat = sem("ln_stat")
        ln_agg = sem("ln_agg")
        ln_var = sem("ln_var")
        ln_rstd = sem("ln_rstd")
        ln_out = sem("ln_out")
        hin_tr = sem("hin_tr")
        hin_mod = sem("hin_mod")
        hin_hi = sem("hin_hi")
        hin_lo = sem("hin_lo")
        ab_split = sem("ab_split")
        ab_mm = sem("ab_mm")
        gate_step = sem("gate_step")
        gate_act = sem("gate_act")
        cum_mm = sem("cum_mm")
        gate_done = sem("gate_done")
        proj = sem("proj")
        conv_tap = sem("conv_tap")
        conv = sem("conv")
        silu = sem("silu")
        z_done = sem("z_done")
        sq_done = sem("sq_done")
        ssq = sem("ssq")
        rr_done = sem("rr_done")
        rn_done = sem("rn_done")
        tr = sem("tr")
        kn = sem("kn")
        trb = sem("trb")
        knt = sem("knt")
        vev = sem("vev")
        gst_done = sem("gst_done")
        gbc = sem("gbc")
        egc = sem("egc")
        dm = sem("dm")
        edm = sem("edm")
        kd_done = sem("kd_done")
        kts = sem("kts")
        kk = sem("kk")
        lt = sem("lt")
        att_done = sem("att_done")
        n1 = sem("n1")
        nn = sem("nn")
        xy = sem("xy")
        x_done = sem("x_done")
        y_done = sem("y_done")
        ks = sem("ks")
        res = sem("res")
        solve = sem("solve")
        vn = sem("vn")
        kdv = sem("kdv")
        state = sem("state")
        o_done = sem("o_done")
        sqo = sem("sqo")
        ssqo = sem("ssqo")
        ro_done = sem("ro_done")
        rno_done = sem("rno_done")
        rst_done = sem("rst_done")
        rbc_mm = sem("rbc_mm")
        rbc_done = sem("rbc_done")
        on_done = sem("on_done")
        dn_done = sem("dn_done")
        ld_dft, ld_res, ld_gb, ld_sk = sem("ld_dft"), sem("ld_res"), sem("ld_gb"), sem("ld_sk")
        f_mm = sem("f_mm")
        f_ev = sem("f_ev")
        fab_mm = sem("fab_mm")
        fab_ev = sem("fab_ev")
        fy_mm = sem("fy_mm")
        fy_h = sem("fy_h")
        fy_l = sem("fy_l")
        four_mm = sem("four_mm")
        four_ev = sem("four_ev")
        dnh = sem("dnh")
        dnl = sem("dnl")
        mer_mm = sem("mer_mm")
        sig = sem("sig")
        mer_v = sem("mer_v")
        mgh = sem("mgh")
        mgl = sem("mgl")
        out_mm = sem("out_mm")
        yt_done = sem("yt_done")
        ytr = sem("ytr")
        x1_sum = sem("x1_sum")
        ln_gain = sem("ln_gain")
        ln_bias = sem("ln_bias")
        h2_tr = sem("h2_tr")
        h2_mod = sem("h2_mod")
        h2_hi = sem("h2_hi")
        h2_lo = sem("h2_lo")
        q_mm = sem("q_mm")
        q_ev = sem("q_ev")
        s_mm = sem("s_mm")
        s_ev = sem("s_ev")
        tk = sem("tk")
        tk_out = sem("tk_out")
        cd = sem("cd")
        cd_exp = sem("cd_exp")
        cd_out = sem("cd_out")
        e_tr = sem("e_tr")
        e_ev = sem("e_ev")
        oh_done = sem("oh_done")
        g_mm = sem("g_mm")
        g_ev = sem("g_ev")
        gs_st = sems("gs_st", 2)
        gu_st = sems("gu_st", 2)
        gq_full = sems("gq_full", 2)
        gl_full = sems("gl_full", 2)
        a_mm = sem("a_mm")
        gelu = sem("gelu")
        cf_done = sem("cf_done")
        ch = sem("ch")
        cl = sem("cl")
        v_mm = sem("v_mm")
        fin = sem("fin")
        fin_tr = sem("fin_tr")
        xo_sum = sem("xo_sum")
        st_out = sem("st_out")

        def units(t):
            return t[:, :, :].rearrange("p (g d c) n -> p g d c n", g=NG, d=NDIR)

        def unit(d, chunk):
            return (chunk // 2) * 4 + d * 2 + chunk % 2

        def walk(d):
            return [*range(NCH)] if d == 0 else [*range(CT - 1, -1, -1), *range(NCH - 1, CT - 1, -1)]

        def first_ada(m):
            return ada_b[:, m - 8, :] if 8 <= m < 12 else ada_a[:, m % 12, :]

        def per_head(t, h):
            return t[:, bass.ds(h * NU, NU)]

        P_BANK = (0, 7, 1, 0, 7, 1)

        def mm3(out, hi, lo, rh, rl, start, stop):
            nc.tensor.matmul(out, hi, rh, start=start, stop=False)
            nc.tensor.matmul(out, hi, rl, start=False, stop=False)
            return nc.tensor.matmul(out, lo, rh, start=False, stop=stop)

        def w_block(slot, k):
            c = slice(k * P, (k + 1) * P)
            return w_hi[:, slot, c], w_lo[:, slot, c]

        block = stack.enter_context(nc.Block())

        @block.sync
        def _(sp_):
            def load_w(n, slot):
                sp_.dma_start(raw[:, slot, :], A["w"][n]).then_inc(raw_full[slot], 16)

            def load_ada(m, slot):
                sp_.dma_start(ada[:, slot, :], A["w_ada"][m]).then_inc(ada_full[slot], 16)

            sp_.dma_start(cond[:, :, :], A["cond"]).then_inc(ld_cond, 16)
            sp_.dma_start(b_ada[:, :], A["b_ada"]).then_inc(ld_cond, 16)
            for t in range(NCH):
                src = A["ctx"][t * P:(t + 1) * P, :] if t < CT else A["x"][(t - CT) * P:(t - CT + 1) * P, :]
                sp_.dma_start(xin[:, t, :], src).then_inc(ld_x[t], 16)
                for m in range(2 * t, 2 * t + 2):
                    sp_.dma_start(first_ada(m), A["w_ada"][m]).then_inc(ada_in[m // 4], 16)
            sp_.dma_start(cst[:, :], A["cst"]).then_inc(ld_cst, 16)
            sp_.dma_start(ab_w[:, :, :], A["ab_w"]).then_inc(ld_ab, 16)
            sp_.dma_start(dtb[:, :], A["dtb"].partition_broadcast(P)).then_inc(ld_ab, 16)
            sp_.dma_start(alog[:, :], A["alog"].partition_broadcast(P)).then_inc(ld_ab, 16)
            sp_.dma_start(cw[:, :, :], A["cw"]).then_inc(ld_head, 16)
            sp_.dma_start(nrm_w[:, :], A["nrm_w"]).then_inc(ld_head, 16)
            for m in range(12, ADA_FIRST):
                sp_.wait_ge(ada_mm, m - 11)
                sp_.dma_start(first_ada(m), A["w_ada"][m]).then_inc(ada_in[m // 4], 16)
            load_w(0, 0)
            load_w(1, 1)
            for j in range(4):
                sp_.wait_ge(split_done, j + 1)
                load_w(j + 2, j % 2)
            with sp_.Fori(0, H) as h:
                for j in range(4):
                    sp_.wait_ge(split_done, h * 4 + (j + 5))
                    load_w(h * 4 + (j + 6), j % 2)
                    sp_.wait_ge(ada_mm, h * 4 + (ADA_FIRST + j - 1))
                    load_ada(h * 4 + (ADA_FIRST + j), j % 2)
            def next_w(i, n):
                sp_.wait_ge(split_done, i + (n + 1))
                load_w(i + (n + 2), n % 2)

            def store_gu(i, x):
                sp_.wait_ge(gelu, i + (x + 1))
                sp_.dma_start(gu_dram[i + x], gu[:, x % 2, :]).then_inc(gu_st[x % 2], 16)

            with sp_.Fori(2, (T_QUERY - T_F) // 2) as i:
                for j in range(2):
                    next_w(i * 2, T_F + j)
            for j in range(4):
                next_w(0, T_QUERY + j)
            with sp_.Fori(1, PH) as i:
                for j in range(4):
                    next_w(i * 4, T_QUERY + j)
                    if j % 2:
                        store_gu(i * 2 - 2, j // 2)
            for j in range(4):
                next_w(0, T_U + j)
                if j % 2:
                    store_gu(0, 2 * PH - 2 + j // 2)
            with sp_.Fori(1, (PK - 2 * PH) // 4) as i:
                for j in range(4):
                    next_w(i * 4, T_U + j)
                    store_gu(i * 4 + (2 * PH - 4), j)

            def load_gl(q, slot):
                sp_.dma_start(gl[:, slot, :, :], gu_dram.rearrange("(q i) p t -> q p i t", i=4)[q]).then_inc(gl_full[slot], 16)

            def load_gq(q, slot):
                sp_.dma_start(gq[:, slot, :, :, :].rearrange("p g i t -> p g (i t)"),
                              g_dram.rearrange("g j (q i) t -> q j g (i t)", i=4)[q]).then_inc(gq_full[slot], 16)

            for j in range(2):
                load_gl(j, j)
            for j in range(2):
                sp_.wait_ge(gs_st[j], SEQ // GTOK // 2 * 16)
            for j in range(2):
                load_gq(j, j)
            for j in range(4):
                next_w(0, T_V + j)
                store_gu(0, PK - 4 + j)

            def v_loads(r_, y0, first, last):
                for y in range(y0, 8):
                    if not last or y < 6:
                        next_w(r_ * 8, T_V + y)
                    if y == 1 and not first:
                        sp_.wait_ge(cf_done, r_ * 8)
                        load_gl(r_ * 2 + 1, 1)
                        load_gq(r_ * 2 + 1, 1)
                    if y == 5 and first:
                        for j in range(2):
                            sp_.wait_ge(gu_st[j], PK // 2 * 16)
                    if y == 5 and not last:
                        sp_.wait_ge(cf_done, r_ * 8 + 4)
                        load_gl(r_ * 2 + 2, 0)
                        load_gq(r_ * 2 + 2, 0)

            v_loads(0, 4, True, False)
            with sp_.Fori(1, N_IT) as r_:
                v_loads(r_, 0, False, False)
            v_loads(N_IT, 0, False, True)
            for b in range(LAT):
                sp_.wait_ge(ln_bias, LAT + b + 1)
                sp_.dma_start(A["out"][b * P:(b + 1) * P, :], xo[:, b, :]).then_inc(st_out, 16)
            sp_.wait_ge(st_out, LAT * 16)

        @block.scalar
        def _(act):
            def hi(n, i, m, slot):
                act.wait_ge(raw_full[slot % RAW], (i * m[0] + m[1]) * 16)
                nc.scalar.copy(w_hi[:, slot, :], raw[:, slot % RAW, :]).then_inc(hi_done, 1)

            act.wait_ge(ld_cond, 32)
            nc.scalar.activation(cond_s[:, :, :], cond[:, :, :], ACT.Silu).then_inc(cond_done, 1)
            act.wait_ge(ld_ab, 48)
            nc.scalar.copy(ab_hi[:, :, :], ab_w[:, :, :]).then_inc(ab_split, 1)
            nc.scalar.activation(expa[:, :], alog[:, :], ACT.Exp).then_inc(gate_act, 1)
            act.wait_ge(mods_done, 2)
            for k in range(KB):
                act.wait_ge(hin_tr, k + 1)
                if k >= 2:
                    act.wait_ge(hin_lo, 2 * (k - 1))
                for s, (src, n0, n1_) in enumerate(((bank[k % 2][:, :], CTX, CTX + SEQ),
                                                    (bank[2 + k % 2][:, 0:CTX], 0, CTX))):
                    nc.scalar.activation(hm[:, k % 2, n0:n1_], src, ACT.Identity, bias=mods[:, k, s:s + 1],
                                         scale=mods[:, KB + k, s:s + 1]).then_inc(hin_mod, 1)
                act.wait_ge(hin_mod, 2 * k + 2)
                nc.scalar.copy(lat_hi[:, k, :], hm[:, k % 2, CTX:]).then_inc(hin_hi, 1)
                nc.scalar.copy(ctx_hi[:, k, :], hm[:, k % 2, 0:CTX]).then_inc(hin_hi, 1)
            for j in range(RING):
                hi(j, 0, (0, j // 2 + 1), j)
            act.wait_ge(ab_mm, 2)
            nc.scalar.copy(abT[0:32, CTX:], bank[4][0:32, :]).then_inc(ab_split, 1)
            nc.scalar.copy(abT[0:32, 0:CTX], bank[5][0:32, 0:CTX]).then_inc(ab_split, 1)
            act.wait_ge(gate_step, 5)
            nc.scalar.activation(sp[3][:, :], sp[2][:, :], ACT.Exp).then_inc(gate_act, 1)
            nc.scalar.activation(sp[4][:, :], sp[1][:, :], ACT.Exp, scale=-1.0).then_inc(gate_act, 1)
            act.wait_ge(gate_done, 4)
            nc.scalar.activation(kds[:, :], sp[17][:, :], ACT.Exp).then_inc(gate_act, 1)
            act.wait_ge(cum_mm, 3)
            nc.scalar.activation(egl[:, :], bank[5][:, H * NU:2 * H * NU], ACT.Exp).then_inc(gate_act, 1)

            def activations(h):
                for o, (dst, a, b) in enumerate(((kT, CTX, CTX + SEQ), (kT, 0, CTX),
                                                 (vT, CTX, CTX + SEQ), (vT, 0, CTX), (qT, 0, SEQ))):
                    act.wait_ge(conv, h * 5 + (o + 1))
                    nc.scalar.activation(dst[:, a:b], cv[:, o % 2, 0:b - a], ACT.Silu).then_inc(silu, 1)
                    if o in (1, 3, 4):
                        j = o // 2
                        hi(None, h, (2, 3 + j // 2), j)
                act.wait_ge(proj, h * 6 + 6)
                hi(None, h, (2, 4), 3)
                nc.scalar.activation(dn[:, bass.ds(h, 1), :].rearrange("p o n -> p (o n)"), bank[1][:, :], ACT.Silu).then_inc(z_done, 1)
                act.wait_ge(silu, h * 5 + 5)
                nc.scalar.activation(sqv[:, 0:NCH * P], kT[:, :], ACT.Square).then_inc(sq_done, 1)
                nc.scalar.activation(sqv[:, NCH * P:NCH * P + SEQ], qT[:, :], ACT.Square).then_inc(sq_done, 1)

            def exp_decay(h):
                for g in range(NG):
                    act.wait_ge(gbc, h * 3 + (g + 1))
                    nc.scalar.activation(eN[:, 4 * g:4 * g + 4, :].rearrange("p a b -> p (a b)"), bank[5 + g][:, :],
                                         ACT.Exp).then_inc(egc, 1)

            def act_head(h, more):
                act.wait_ge(trb, h * 2 + 1)
                nc.scalar.copy(knT[:, 0:512], bank[2][:, :]).then_inc(knt, 1)
                nc.scalar.copy(knT[:, 512:], bank[3][:, 0:CTX]).then_inc(knt, 1)
                act.wait_ge(trb, h * 2 + 2)
                nc.scalar.copy(qnT[:, :], bank[4][:, :]).then_inc(knt, 1)
                for g in range(NG):
                    act.wait_ge(dm, h * 12 + 4 * (g + 1))
                    v = dY[:, 4 * g:4 * g + 4, :].rearrange("p a b -> p (a b)")
                    nc.scalar.activation(v, v, ACT.Exp).then_inc(edm, 1)
                act.wait_ge(tr, h * 3 + 3)
                nc.scalar.copy(Vt[:, 0:4, :].rearrange("p a b -> p (a b)"), bank[5][:, :]).then_inc(vev, 1)
                nc.scalar.copy(Vt[:, 4:6, :].rearrange("p a b -> p (a b)"), bank[6][:, 0:CTX]).then_inc(vev, 1)
                if more:
                    activations(h + 1)
                act.wait_ge(o_done, h + 1)
                nc.scalar.activation(cv[:, 1, :], bank[2][:, :], ACT.Square).then_inc(sqo, 1)
                if more:
                    exp_decay(h + 1)
                act.wait_ge(rbc_mm, h + 1)
                nc.scalar.copy(rbc, bank[4][:, :]).then_inc(rbc_done, 1)

            activations(0)
            exp_decay(0)
            with act.Fori(0, H - 1) as h:
                act_head(h, True)
            act_head(H - 1, False)

            def hi_n(q, i=0, per=0):
                act.wait_ge(raw_full[q % RAW], i * (per // 2 * 16) + (q // 2 + 1) * 16)
                nc.scalar.copy(w_hi[:, q % RING, :], raw[:, q % RAW, :]).then_inc(hi_done, 1)

            act.wait_ge(dn_done, H)
            act.dma_start(dft[:, :, :, :], A["dft"]).then_inc(ld_dft, 16)
            for m in range(FG):
                act.wait_ge(f_mm, m + 1)
                nc.scalar.copy(fT[:, m, :], bank[m % 2][:, :]).then_inc(f_ev, 1)
                hi_n(T_F + RING + m)
            for m in range(FG):
                act.wait_ge(fy_mm, m + 1)
                nc.scalar.copy(fy_hi[:, m, :], bank[6 + m % 2][:, :]).then_inc(fy_h, 1)
            for m in range(H):
                nc.scalar.copy(dn_hi[:, m, :], dn[:, m, :]).then_inc(dnh, 1)
            for m in range(KB):
                act.wait_ge(four_mm, m + 1)
                nc.scalar.copy(fourT[:, m, :], bank[m % 2][:, :]).then_inc(four_ev, 1)
                if m % 2:
                    hi_n(T_FOUR + RING + m // 2)
            act.wait_ge(dnl, H)
            act.dma_start(x1[:, :, :], A["x"].rearrange("(b p) n -> p b n", p=P)).then_inc(ld_res, 16)
            with act.Fori(0, 2) as i:
                for m in range(4):
                    for t in range(2):
                        act.wait_ge(mer_v, i * 12 + (3 * m))
                        act.wait_ge(mer_mm, i * 12 + (3 * m + t + 1))
                        nc.scalar.activation(sg[:, t, :], bank[3 * (m % 2) + t][:, :], ACT.Sigmoid).then_inc(sig, 1)
                        hi_n(T_MERGE + RING + 3 * m + t, i, 12)
                    act.wait_ge(mer_v, i * 12 + (3 * m + 3))
                    nc.scalar.copy(mg_hi[:, bass.ds(i * 4 + m, 1), :], ma[:, 2:3, :]).then_inc(mgh, 1)
                    hi_n(T_MERGE + RING + 3 * m + 2, i, 12)
            act.wait_ge(mgl, KB)
            act.dma_start(gb[:, 0, :], A["ln"][0].partition_broadcast(P)).then_inc(ld_gb, 16)
            act.dma_start(gb[:, 1, :], A["ln"][2].partition_broadcast(P)).then_inc(ld_gb, 16)
            for m in range(KB):
                act.wait_ge(out_mm, m + 1)
                nc.scalar.activation(yT[:, m, :], bank[m % 2][:, :], ACT.Copy,
                                     scale=mods[:, 2 * KB + m, 0:1]).then_inc(yt_done, 1)
                hi_n(T_OUT + RING + m)
            for k in range(KB):
                act.wait_ge(h2_tr, k + 1)
                if k >= 2:
                    act.wait_ge(h2_lo, k - 1)
                nc.scalar.activation(h2[:, k % 2, :], bank[k % 2][:, :], ACT.Identity, bias=mods[:, 3 * KB + k, 0:1],
                                     scale=mods[:, 4 * KB + k, 0:1]).then_inc(h2_mod, 1)
                act.wait_ge(h2_mod, k + 1)
                nc.scalar.copy(lat_hi[:, k, :], h2[:, k % 2, :]).then_inc(h2_hi, 1)
            act.wait_ge(h2_lo, KB)
            act.dma_start(sk[:, :, :], A["sub_keys"]).then_inc(ld_sk, 16)
            def act_u(i, per, x):
                act.wait_ge(a_mm, i * per + (x + 1))
                act.wait_ge(gu_st[x % 2], i * (per * 8) + x // 2 * 16)
                nc.scalar.activation(gu[:, x % 2, :], bank[6 + x % 2][:, :], ACT.Gelu).then_inc(gelu, 1)

            with act.Fori(0, 2 * PH // 4) as i:
                for j in range(4):
                    act.wait_ge(q_mm, i * 4 + (j + 1))
                    nc.scalar.copy(qq[:, j, :], bank[j % 2][:, :]).then_inc(q_ev, 1)
                    hi_n(T_QUERY + RING + 2 * j, i, 8)
                    act_u(i, 4, j)
                    hi_n(T_QUERY + RING + 2 * j + 1, i, 8)
                    act.wait_ge(tk, i * (4 * TK_N) + max(TK_N * (j - 1), 0))
                    act.wait_ge(s_mm, i * 4 + (j + 1))
                    nc.scalar.copy(sc[:, j % 2, :, :].rearrange("p a b -> p (a b)"), bank[2 + j % 2][:, :]).then_inc(s_ev, 1)
            with act.Fori(0, LAT) as b:
                for j in range(U_CD):
                    act_u(b, U_CD, X_CD + j)
                    hi_n(T_U + RING + j, b, U_CD)
                act.wait_ge(cd, b * CD_N + CD_EXP)
                nc.scalar.activation(bf[5][:, :, :], bf[4][:, :, :], ACT.Exp).then_inc(cd_exp, 1)
                act.wait_ge(e_tr, b + 1)
                nc.scalar.copy(eidT[:, :, bass.ds(b * P, P)], bank[4][:, 0:3 * P].rearrange("p (a b) -> p a b", a=3)).then_inc(e_ev, 1)
            with act.Fori(0, SEQ // GTOK // 2) as i:
                for j in range(2):
                    act.wait_ge(gs_st[j], i * 16)
                    with act.Fori(0, GTOK // 32) as t:
                        for w in range(4):
                            for z in range(2):
                                act.wait_ge(g_mm, i * (2 * GTOK // 4) + t * 8 + (j * GTOK // 4 + 2 * w + z + 1))
                                nc.scalar.copy(gs[:, j, :, bass.ds(t * 32 + (8 * w + 4 * z), 4)].rearrange("p i t -> p t i"),
                                               bank[z][:, :].rearrange("p (t i) -> p t i", t=4)).then_inc(g_ev, 1)
                            x = i * (2 * GTOK // 8) + t * 4
                            act.wait_ge(a_mm, x + (X_G + j * (GTOK // 8) + w + 1))
                            act.wait_ge(gu_st[w % 2], x * 8 + (X_G + j * (GTOK // 8) + w) // 2 * 16)
                            nc.scalar.activation(gu[:, w % 2, :], bank[6 + w % 2][:, :], ACT.Gelu).then_inc(gelu, 1)
                            n = T_U + X_G - 2 * PH + j * (GTOK // 8) + RING + w
                            act.wait_ge(raw_full[n % RAW], x * 8 + (n // 2 + 1) * 16)
                            nc.scalar.copy(w_hi[:, n % RING, :], raw[:, n % RAW, :]).then_inc(hi_done, 1)
                    act.wait_ge(g_ev, i * (2 * GTOK // 4) + (j + 1) * (GTOK // 4))
                    act.dma_start(g_dram[i * 2 + j], gs[:, j, :, :]).then_inc(gs_st[j], 16)
            def act_c(i, y):
                act.wait_ge(cf_done, i + (y + 1))
                nc.scalar.copy(c_hi[:, y % 4, :], cf[:, y % 2, :]).then_inc(ch, 1)

            for x in range(X_END, PK):
                if x == PK - 2:
                    for j in range(2):
                        act.wait_ge(gs_st[j], SEQ // GTOK // 2 * 16)
                    act.dma_start(gb2[:, 0, :], A["ln"][1].partition_broadcast(P)).then_inc(ld_gb, 16)
                    act.dma_start(gb2[:, 1, :], A["ln"][3].partition_broadcast(P)).then_inc(ld_gb, 16)
                    for y in range(4):
                        act_c(0, y)
                act_u(0, 0, x)
                hi_n(T_U - 2 * PH + x + RING)

            with act.Fori(0, PK // 4 - 1) as i:
                for y in range(4):
                    act.wait_ge(v_mm, i * 4 + (y + 1))
                    act_c(i * 4, y + 4)
                    hi_n(T_V + RING + y, i, 4)
            act.wait_ge(v_mm, PK)
            for k in range(KB):
                nc.scalar.activation(acc[:, k, :], bank[k][:, :], ACT.Copy, scale=mods[:, 5 * KB + k, 0:1]).then_inc(fin, 1)

        @block.gpsimd
        def _(pool):
            def lo(slot, *count):
                pool.wait_ge(hi_done, *count)
                nc.gpsimd.tensor_sub(w_lo[:, slot, :], raw[:, slot % RAW, :],
                                     w_hi[:, slot, :].bitcast(F32)).then_inc(split_done, 1)

            nc.gpsimd.memset(nhalf[:, :], -0.5).then_inc(nhalf_set, 1)
            pool.wait_ge(nhalf_set, 1)
            pool.wait_ge(ln_var, 1)
            nc.gpsimd.tensor_tensor(rstd[:, :], vare[:, :], nhalf[:, 0:NCH], ALU.pow).then_inc(ln_rstd, 1)
            for j in range(RING):
                lo(j, j + 1)
            for j in range(4):
                lo(j, 5 + j)

            def inverse_norms(h):
                pool.wait_ge(rr_done, h * 2 + 2)
                nc.gpsimd.tensor_tensor(rn[:, 0:NCH + LAT], rr[:, 0, 0:NCH + LAT], nhalf[:, 0:NCH + LAT],
                                        ALU.pow).then_inc(rn_done, 1)

            inverse_norms(0)

            def pool_head(h, more):
                pool.wait_ge(dn_done, h)
                pool.wait_ge(knt, h * 3 + 2)
                pool.wait_ge(egc, h * 3 + 3)
                e4 = eN[:, :, :].rearrange("p (g d c) n -> p g d (c n)", g=NG, d=NDIR)
                k4 = kTs[:, :, :].rearrange("p (g d c) n -> p g d (c n)", g=NG, d=NDIR)
                for d in range(NDIR):
                    nc.gpsimd.tensor_mul(k4[:, :, d, :], knT[:, :].rearrange("p (g n) -> p g n", g=NG),
                                         e4[:, :, d, :]).then_inc(kts, 1)
                pool.wait_ge(knt, h * 3 + 3)
                for d in range(NDIR):
                    nc.gpsimd.tensor_mul(qTs[:, :, d, :], qnT[:, :].rearrange("p (g n) -> p g n", g=2),
                                         e4[:, 1:NG, d, :]).then_inc(kts, 1)
                pool.wait_ge(kn, h * 3 + 2)
                for d in range(NDIR):
                    scale = per_head(kds, h).rearrange("p (g d c) -> p g d c", g=NG, d=NDIR)[:, :, d, :]
                    nc.gpsimd.tensor_mul(units(Kd)[:, :, d, :, :],
                                         Kn[:, :, :].rearrange("p (g c) n -> p g c n", g=NG),
                                         bc(scale, P)).then_inc(kd_done, 1)
                if more:
                    for j in range(2):
                        lo(j, h * 4 + (9 + j))
                pool.wait_ge(ro_done, h + 1)
                nc.gpsimd.tensor_tensor(rno[:, :], ro[:, :], nhalf[:, 0:LAT], ALU.pow).then_inc(rno_done, 1)
                if more:
                    inverse_norms(h + 1)
                pool.wait_ge(rno_done, h + 1)
                nc.gpsimd.tensor_mul(rst, bc(rno[:, :], P), rep(ones, LAT)).then_inc(rst_done, 1)
                if more:
                    for j in range(2, 4):
                        lo(j, h * 4 + (9 + j))

            with pool.Fori(0, H - 1) as h:
                pool_head(h, True)
            pool_head(H - 1, False)

            with pool.Fori(0, (T_QUERY - T_F) // 4) as i:
                for j in range(4):
                    lo(j, i * 4 + (T_F + RING + 1 + j))
            for n_norm in (1, 2):
                pool.wait_ge(ln_var, n_norm + 1)
                nc.gpsimd.tensor_tensor(rstd[:, 0:LAT], vare[:, 0:LAT], nhalf[:, 0:LAT], ALU.pow).then_inc(ln_rstd, 1)
            with pool.Fori(0, (T_ALL - T_QUERY - RING) // 4) as i:
                for j in range(4):
                    lo(j, i * 4 + (T_QUERY + RING + 1 + j))
            pool.wait_ge(ln_var, 4)
            nc.gpsimd.tensor_tensor(rstd[:, 0:LAT], vare[:, 0:LAT], nhalf[:, 0:LAT], ALU.pow).then_inc(ln_rstd, 1)

        @block.vector
        def _(dve):
            steps = [0]

            def link(ins):
                steps[0] += 1
                ins.then_inc(gate_step, 1)
                dve.wait_ge(gate_step, steps[0])

            for t in range(NCH):
                dve.wait_ge(ld_x[t], 16)
                for i in range(2):
                    nc.vector.bn_stats(stats[:, t, i, :], xin[:, t, i * 512:(i + 1) * 512]).then_inc(ln_stat, 1)
            for t in range(NCH):
                dve.wait_ge(ln_stat, 2 * t + 2)
                nc.vector.bn_aggr(mv[:, t, :], stats[:, t, :, :]).then_inc(ln_agg, 1)
            dve.wait_ge(ln_agg, NCH)
            nc.vector.tensor_scalar(vare[:, :], mv[:, :, 1], LN_EPS, None, ALU.add).then_inc(ln_var, 1)
            dve.wait_ge(ln_rstd, 1)
            for t in range(NCH):
                nc.vector.tensor_scalar(xin[:, t, :], xin[:, t, :], mv[:, t, 0:1], rstd[:, t:t + 1],
                                        ALU.subtract, ALU.mult).then_inc(ln_out, 1)
            dve.wait_ge(ada_mm, ADA_FIRST)
            nc.vector.tensor_tensor(mods[:, 0:ADA_FIRST, :],
                                    bank[7][:, 0:2 * ADA_FIRST].rearrange("p (a b) -> p a b", b=2),
                                    bc(b_ada[:, 0:ADA_FIRST], 2), ALU.add).then_inc(mods_done, 1)
            dve.wait_ge(mods_done, 1)
            nc.vector.tensor_scalar(mods[:, KB:2 * KB, :], mods[:, KB:2 * KB, :], 1.0, None,
                                    ALU.add).then_inc(mods_done, 1)
            dve.wait_ge(ab_split, 1)
            nc.vector.tensor_sub(ab_lo[:, :, :], ab_w[:, :, :], ab_hi[:, :, :].bitcast(F32)).then_inc(ab_split, 1)
            for k in range(KB):
                dve.wait_ge(hin_hi, 2 * k + 2)
                nc.vector.tensor_sub(lat_lo[:, k, :], hm[:, k % 2, CTX:],
                                     lat_hi[:, k, :].bitcast(F32)).then_inc(hin_lo, 1)
                nc.vector.tensor_sub(ctx_lo[:, k, :], hm[:, k % 2, 0:CTX],
                                     ctx_hi[:, k, :].bitcast(F32)).then_inc(hin_lo, 1)
            dve.wait_ge(ab_mm, 3)
            dve.wait_ge(ld_ab, 48)
            abp = bank[6][:, 0:NCH * 32].rearrange("p (g c e d h) -> p e d h g c", g=NG, c=2, e=2, d=NDIR)

            def gv(t):
                return t[:, :].rearrange("p (h g d c) -> p d h g c", h=H, g=NG, d=NDIR)

            def over_units(t, d):
                return bc(bc(t[:, d * H:(d + 1) * H], NG), 2)

            for d in range(NDIR):
                nc.vector.tensor_tensor(gv(sp[0])[:, d], abp[:, 0, d], over_units(dtb, d), ALU.add).then_inc(gate_step, 1)
                nc.vector.tensor_copy(gv(sp[1])[:, d], abp[:, 1, d]).then_inc(gate_step, 1)
            steps[0] = 4
            dve.wait_ge(gate_step, 4)
            link(nc.vector.scalar_tensor_tensor(sp[2][:, :], sp[0][:, :], -1.0, sp[0][:, :], ALU.mult, ALU.min))
            dve.wait_ge(gate_act, 3)
            link(nc.vector.tensor_scalar(sp[5][:, :], sp[3][:, :], 2.0, None, ALU.add))
            link(nc.vector.reciprocal(sp[6][:, :], sp[5][:, :]))
            link(nc.vector.tensor_tensor(sp[7][:, :], sp[3][:, :], sp[6][:, :], ALU.mult))
            link(nc.vector.tensor_tensor(sp[8][:, :], sp[7][:, :], sp[7][:, :], ALU.mult))
            link(nc.vector.tensor_scalar(sp[9][:, :], sp[8][:, :], 1.0 / 17, None, ALU.mult))
            cur = 9
            for c in (15, 13, 11, 9, 7, 5, 3):
                link(nc.vector.scalar_tensor_tensor(sp[19 - cur][:, :], sp[cur][:, :], 1.0 / c, sp[8][:, :],
                                                    ALU.add, ALU.mult))
                cur = 19 - cur
            link(nc.vector.scalar_tensor_tensor(sp[11][:, :], sp[cur][:, :], 1.0, sp[7][:, :], ALU.add, ALU.mult))
            link(nc.vector.tensor_scalar(sp[12][:, :], sp[0][:, :], 0.0, None, ALU.max))
            link(nc.vector.scalar_tensor_tensor(sp[13][:, :], sp[11][:, :], 2.0, sp[12][:, :], ALU.mult, ALU.add))
            link(nc.vector.tensor_scalar(sp[14][:, :], sp[13][:, :], -1.0, None, ALU.mult))
            for d in range(NDIR):
                nc.vector.tensor_tensor(gv(gall)[:, d], gv(sp[14])[:, d], over_units(expa, d),
                                        ALU.mult).then_inc(gate_done, 1)
            link(nc.vector.tensor_scalar(sp[15][:, :], sp[4][:, :], 1.0, None, ALU.add))
            nc.vector.reciprocal(beta[:, :], sp[15][:, :]).then_inc(gate_done, 1)
            dve.wait_ge(cum_mm, 3)
            link(nc.vector.tensor_copy(gcum[:, :], bank[5][:, 0:H * NU]))
            nc.vector.tensor_tensor(sp[17][:, :], bank[5][:, H * NU:2 * H * NU], gcum[:, :],
                                    ALU.subtract).then_inc(gate_done, 1)
            dve.wait_ge(gate_act, 5)
            dve.wait_ge(ld_head, 32)
            nc.vector.tensor_copy(sp[16][:, :], beta[:, :]).then_inc(gate_done, 1)

            def convolution(h, o):
                kind, lat = o // 2, o % 2 == 0
                n_row, row = (SEQ // GRID_W, GRID_W) if lat else (1, CTX)
                src = bank[P_BANK[o]][:, 0:n_row * row].rearrange("p (r n) -> p r n", r=n_row)
                dst = cv[:, o % 2, 0:n_row * row].rearrange("p (r n) -> p r n", r=n_row)
                dve.wait_ge(silu, h * 5 + max(o - 1, 0))
                dve.wait_ge(proj, h * 6 + (o + 1))

                def tap(t):
                    return cw[:, t, bass.ds(h + kind * H, 1)]

                nc.vector.tensor_scalar(dst, src, tap(TAPS // 2), None, ALU.mult).then_inc(conv_tap, 1)
                others = [t for t in range(TAPS) if t != TAPS // 2]
                for n, t in enumerate(others):
                    s = t - TAPS // 2
                    a, b = max(0, -s), row - max(0, s)
                    dve.wait_ge(conv_tap, h * 20 + (4 * o + n + 1))
                    nc.vector.scalar_tensor_tensor(dst[:, :, a:b], src[:, :, a + s:b + s], tap(t), dst[:, :, a:b],
                                                   ALU.mult, ALU.add).then_inc(conv if n == 3 else conv_tap, 1)

            def decays(h):
                nc.vector.tensor_copy(gst[:, :, :], bc(per_head(gall, h), P)).then_inc(gst_done, 1)

            def square_norms(h):
                dve.wait_ge(ssq, h + 1)
                nc.vector.tensor_scalar(rr[:, 0, 0:NCH], bank[3][:, LAT:LAT + NCH], L2_EPS, None,
                                        ALU.add).then_inc(rr_done, 1)
                nc.vector.tensor_scalar(rr[:, 0, NCH:NCH + LAT], bank[3][:, LAT + NCH:LAT + NCH + LAT], float(P),
                                        P * L2_EPS, ALU.mult, ALU.add).then_inc(rr_done, 1)

            def dve_head(h, more):
                dve.wait_ge(tr, h * 3 + 1)
                dve.wait_ge(kd_done, h * 2)
                dve.wait_ge(rn_done, h + 1)
                b4 = "p (a b) -> p a b"
                nc.vector.tensor_tensor(Kn[:, 0:4, :], bank[0][:, :].rearrange(b4, b=P), bc(rn[:, 0:4], P),
                                        ALU.mult).then_inc(kn, 1)
                nc.vector.tensor_tensor(Kn[:, 4:6, :], bank[1][:, 0:CTX].rearrange(b4, b=P), bc(rn[:, 4:6], P),
                                        ALU.mult).then_inc(kn, 1)
                dve.wait_ge(tr, h * 3 + 2)
                nc.vector.tensor_tensor(Qn[:, :, :], bank[4][:, :].rearrange(b4, b=P), bc(rn[:, 6:10], P),
                                        ALU.mult).then_inc(kn, 1)
                for g in range(NG):
                    dve.wait_ge(egc, h * 3 + (g + 1))
                    for q in range(4):
                        u = 4 * g + q
                        nc.vector.scalar_tensor_tensor(dY[:, u, :], bank[5 + g][:, q * P:(q + 1) * P],
                                                       gcum[:, bass.ds(h * NU + u, 1)], neg_dir(q // 2),
                                                       ALU.subtract, ALU.min).then_inc(dm, 1)
                dve.wait_ge(kk, h * 2 + 1)
                for g in range(NG):
                    dve.wait_ge(edm, h * 3 + (g + 1))
                    for q in range(4):
                        u, c = 4 * g + q, 2 * g + q % 2
                        nc.vector.scalar_tensor_tensor(Lt[:, u, :], bank[2 + c // 4][:, (c % 4) * P:(c % 4 + 1) * P],
                                                       beta[:, bass.ds(h * NU + u, 1)], dY[:, u, :],
                                                       ALU.mult, ALU.mult).then_inc(lt, 1)
                dve.wait_ge(kk, h * 2 + 2)
                d4 = dY[:, :, :].rearrange("p (g d c) n -> p g d (c n)", g=NG, d=NDIR)
                for g in range(2):
                    nc.vector.tensor_tensor(att[:, g, :, :], rep(bank[4][:, g * 256:(g + 1) * 256], NDIR),
                                            d4[:, g + 1, :, :], ALU.mult).then_inc(att_done, 1)

                dve.wait_ge(ada_mm, h * 4 + (ADA_FIRST + 4))
                nc.vector.tensor_tensor(mods[:, bass.ds(h * 4 + ADA_FIRST, 4), :],
                                        bank[0][:, 0:8].rearrange("p (a b) -> p a b", b=2),
                                        bc(b_ada[:, bass.ds(h * 4 + ADA_FIRST, 4)], 2), ALU.add).then_inc(mods_done, 1)

                def masked(h, lv, base):
                    for g in range(NG):
                        dve.wait_ge(n1, base + (g + 1))
                        m = cst[:, bass.ds(lv * (2 * P) + C_LVL, 2 * P)].rearrange("p (d n) -> p d n", d=NDIR)
                        m = m.unsqueeze(2).to_broadcast([P, NDIR, 2, P])
                        nc.vector.tensor_tensor(units(eN)[:, g], bank[2 + g][:, :].rearrange(
                            "p (d c n) -> p d c n", d=NDIR, c=2), m, ALU.mult).then_inc(nn, 1)

                dve.wait_ge(kts, h * 4 + 4)
                masked(h, 0, h * 21)
                id4 = rep(ident, 4)
                for g in range(NG):
                    u4 = slice(4 * g, 4 * g + 4)
                    dve.wait_ge(nn, h * 21 + (g + 1))
                    nc.vector.tensor_tensor(dY[:, u4, :], eN[:, u4, :], id4, ALU.add).then_inc(y_done, 1)
                    dve.wait_ge(xy, h * 21 + (g + 1))
                    nc.vector.tensor_tensor(gX[:, u4, :], bank[5 + g][:, :].rearrange(b4, b=P), id4,
                                            ALU.add).then_inc(x_done, 1)

                def add_up(base, last):
                    for g in range(NG):
                        u4 = slice(4 * g, 4 * g + 4)
                        dve.wait_ge(xy, base + (g + 1))
                        if not last:
                            nc.vector.tensor_tensor(dY[:, u4, :], dY[:, u4, :], bank[2 + g][:, :].rearrange(b4, b=P),
                                                    ALU.add).then_inc(y_done, 1)
                        nc.vector.tensor_tensor(gX[:, u4, :], gX[:, u4, :], bank[5 + g][:, :].rearrange(b4, b=P),
                                                ALU.add).then_inc(x_done, 1)

                with dve.Fori(1, LEVELS - 1) as lv:
                    masked(h, lv, h * 21 + lv * 3)
                    add_up(h * 21 + lv * 3, False)
                masked(h, LEVELS - 1, h * 21 + (LEVELS - 1) * 3)
                add_up(h * 21 + (LEVELS - 1) * 3, True)

                for s in range(NCH):
                    if s:
                        for d in range(NDIR):
                            dve.wait_ge(ks, h * 10 + (2 * (s - 1) + d + 1))
                            nc.vector.tensor_tensor(Rd[:, d, :], Vt[:, walk(d)[s], :], bank[3 + d][:, 0:P],
                                                    ALU.subtract).then_inc(res, 1)
                    for d in range(NDIR):
                        u = unit(d, walk(d)[s])
                        dve.wait_ge(solve, h * 12 + (2 * s + d + 1))
                        nc.vector.tensor_scalar(Vn[:, d, :], bank[5 + d][:, 0:P], beta[:, bass.ds(h * NU + u, 1)],
                                                None, ALU.mult).then_inc(vn, 1)
                    if s < NCH - 1:
                        for d in range(NDIR):
                            u = unit(d, walk(d)[s])
                            dve.wait_ge(kdv, h * 10 + (2 * s + d + 1))
                            new = bank[3 + d][:, 0:P]
                            if s == 0:
                                nc.vector.tensor_copy(St[:, d, 0, :], new).then_inc(state, 1)
                            else:
                                dve.wait_ge(state, h * 10 + (2 * (s - 1) + d + 1))
                                nc.vector.scalar_tensor_tensor(St[:, d, s % 2, :], St[:, d, (s - 1) % 2, :],
                                                               egl[:, bass.ds(h * NU + u, 1)], new,
                                                               ALU.mult, ALU.add).then_inc(state, 1)
                    if more and s:
                        convolution(h + 1, s - 1)
                if more:
                    decays(h + 1)
                dve.wait_ge(ssqo, h + 1)
                if more:
                    dve.wait_ge(ssq, h + 2)
                nc.vector.tensor_scalar(ro[:, :], bank[3][:, 0:LAT], 1.0 / P, RMS_EPS, ALU.mult,
                                        ALU.add).then_inc(ro_done, 1)
                if more:
                    square_norms(h + 1)
                dve.wait_ge(rbc_done, h + 1)
                nc.vector.tensor_tensor(onT, bank[2][:, :], rbc, ALU.mult).then_inc(on_done, 1)
                dve.wait_ge(z_done, h + 1)
                dve.wait_ge(on_done, h + 1)
                o_h = dn[:, bass.ds(h, 1), :].rearrange("p o n -> p (o n)")
                nc.vector.scalar_tensor_tensor(o_h, onT, nrm_w[:, 0:1], o_h, ALU.mult, ALU.mult).then_inc(dn_done, 1)

            for o in range(5):
                convolution(0, o)
            decays(0)
            square_norms(0)
            with dve.Fori(0, H - 1) as h:
                dve_head(h, True)
            dve_head(H - 1, False)
            nc.vector.tensor_scalar(mods[:, 4 * KB:5 * KB, :], mods[:, 4 * KB:5 * KB, :], 1.0, None,
                                    ALU.add).then_inc(mods_done, 1)
            for e in range(2 * FG):
                dve.wait_ge(fab_mm, e + 1)
                nc.vector.tensor_copy(fab[:, e // 2, 2 * (e % 2):2 * (e % 2) + 2, :].rearrange("p a b -> p (a b)"),
                                      bank[2 + e % 4][:, :]).then_inc(fab_ev, 1)
            for m in range(FG):
                dve.wait_ge(fy_h, m + 1)
                nc.vector.tensor_sub(fy_lo[:, m, :], bank[6 + m % 2][:, :], fy_hi[:, m, :].bitcast(F32)).then_inc(fy_l, 1)
            for m in range(H):
                dve.wait_ge(dnh, m + 1)
                nc.vector.tensor_sub(dn_lo[:, m, :], dn[:, m, :], dn_hi[:, m, :].bitcast(F32)).then_inc(dnl, 1)
            dve.wait_ge(four_ev, KB)
            with dve.Fori(0, 2) as i:
                for m in range(4):
                    dve.wait_ge(sig, i * 8 + (2 * m + 1))
                    nc.vector.tensor_tensor(ma[:, 0, :], sg[:, 0, :], fourT[:, bass.ds(i * 4 + m, 1), :].rearrange("p o n -> p (o n)"),
                                            ALU.mult).then_inc(mer_v, 1)
                    dve.wait_ge(sig, i * 8 + (2 * m + 2))
                    dve.wait_ge(mer_mm, i * 12 + (3 * m + 3))
                    nc.vector.tensor_tensor(ma[:, 1, :], sg[:, 1, :], bank[3 * (m % 2) + 2][:, :],
                                            ALU.mult).then_inc(mer_v, 1)
                    dve.wait_ge(mer_v, i * 12 + (3 * m + 2))
                    nc.vector.tensor_tensor(ma[:, 2, :], ma[:, 0, :], ma[:, 1, :], ALU.add).then_inc(mer_v, 1)
                    dve.wait_ge(mgh, i * 4 + (m + 1))
                    nc.vector.tensor_tensor(mg_lo[:, bass.ds(i * 4 + m, 1), :], ma[:, 2:3, :],
                                            mg_hi[:, bass.ds(i * 4 + m, 1), :].bitcast(F32), ALU.subtract).then_inc(mgl, 1)

            def norm(dst, src, n_norm, after_, n_after, gains):
                done = NCH + LAT * (n_norm - 1)
                for t in range(LAT):
                    dve.wait_ge(after_, n_after(t))
                    for i in range(2):
                        nc.vector.bn_stats(stats[:, t, i, :], src[:, t, i * 512:(i + 1) * 512]).then_inc(ln_stat, 1)
                for t in range(LAT):
                    dve.wait_ge(ln_stat, 2 * (done + t) + 2)
                    nc.vector.bn_aggr(mv[:, t, :], stats[:, t, :, :]).then_inc(ln_agg, 1)
                dve.wait_ge(ln_agg, done + LAT)
                nc.vector.tensor_scalar(vare[:, 0:LAT], mv[:, 0:LAT, 1], LN_EPS, None, ALU.add).then_inc(ln_var, 1)
                dve.wait_ge(ln_rstd, n_norm + 1)
                for t in range(LAT):
                    nc.vector.tensor_scalar(dst[:, t, :], src[:, t, :], mv[:, t, 0:1], rstd[:, t:t + 1],
                                            ALU.subtract, ALU.mult).then_inc(ln_out, 1)
                if gains is None:
                    return
                n_gain = LAT * (n_norm // 2)
                for t in range(LAT):
                    dve.wait_ge(ln_out, done + t + 1)
                    nc.vector.tensor_tensor(dst[:, t, :], dst[:, t, :], gains[:, 0, :], ALU.mult).then_inc(ln_gain, 1)
                for t in range(LAT):
                    dve.wait_ge(ln_gain, n_gain + t + 1)
                    nc.vector.tensor_tensor(dst[:, t, :], dst[:, t, :], gains[:, 1, :], ALU.add).then_inc(ln_bias, 1)

            dve.wait_ge(ld_res, 16)
            for t in range(LAT):
                dve.wait_ge(ytr, t + 1)
                for i in range(2):
                    c = slice(i * 512, (i + 1) * 512)
                    nc.vector.scalar_tensor_tensor(x1[:, t, c], x1[:, t, c], ALPHA, bank[2 + 2 * (t % 2) + i][:, :],
                                                   ALU.mult, ALU.add).then_inc(x1_sum, 1)
            dve.wait_ge(ld_gb, 32)
            norm(x1, x1, 1, x1_sum, lambda t: 2 * t + 2, gb)
            norm(xn, x1, 2, ln_bias, lambda t: t + 1, None)
            for k in range(KB):
                dve.wait_ge(h2_hi, k + 1)
                nc.vector.tensor_sub(lat_lo[:, k, :], h2[:, k % 2, :], lat_hi[:, k, :].bitcast(F32)).then_inc(h2_lo, 1)

            def turn(count):
                nc.vector.tensor_copy(mark[:, :], ones[:, 0:1]).then_inc(count, 1)

            def top16(src, cut, vals, ids, n, wait, count):
                turn(count)
                for i in range(n):
                    nc.vector.max(vals[i][:, 0:8], src[i]).then_inc(count, 1)
                wait(n + 1)
                turn(count)
                for i in range(n):
                    nc.vector.max_index(ids[i][:, 0:8], vals[i][:, 0:8], src[i]).then_inc(count, 1)
                    nc.vector.match_replace(cut[i], vals[i][:, 0:8], src[i], -3.0e38).then_inc(count, 1)
                wait(3 * n + 2)
                turn(count)
                for i in range(n):
                    nc.vector.max(vals[i][:, 8:16], cut[i]).then_inc(count, 1)
                wait(4 * n + 3)
                turn(count)
                for i in range(n):
                    nc.vector.max_index(ids[i][:, 8:16], vals[i][:, 8:16], cut[i]).then_inc(count, 1)

            with dve.Fori(0, 2 * PH // 4) as it:
                for j in range(4):
                    dve.wait_ge(s_ev, it * 4 + (j + 1))
                    dve.wait_ge(tk_out, it * 8 + 2 * j)
                    top16([sc[:, j % 2, b, :] for b in range(LAT)], [sc2[:, b, :] for b in range(LAT)],
                          [t16[:, j, b, :] for b in range(LAT)], [i16[:, j, b, :] for b in range(LAT)], LAT,
                          lambda n: dve.wait_ge(tk, it * (4 * TK_N) + (TK_N * j + n)), tk)
                    dve.wait_ge(tk, it * (4 * TK_N) + (TK_N * j + TK_N))
                    o = bass.ds(it * 4 + j, 1)
                    nc.vector.tensor_copy(topv[:, o, :, :], t16[:, j:j + 1, :, :]).then_inc(tk_out, 1)
                    nc.vector.tensor_copy(topi[:, o, :, :], i16[:, j:j + 1, :, :]).then_inc(tk_out, 1)

            dve.wait_ge(tk_out, 4 * PH)
            with dve.Fori(0, LAT) as b:
                made = [0]

                def step(ins):
                    made[0] += 1
                    ins.then_inc(cd, 1)

                def synced():
                    dve.wait_ge(cd, b * CD_N + made[0])

                def side(t, s_):
                    v = t[:, :, bass.ds(b, 1), :].rearrange("p (h s) o k -> p s h (o k)", s=2)
                    return v[:, s_]

                dve.wait_ge(e_tr, b)
                step(nc.vector.tensor_tensor(cand[:, :, :].rearrange("p h (a c) -> p h a c", a=TOPK),
                                             bc(side(topv, 0), TOPK),
                                             side(topv, 1).unsqueeze(2).to_broadcast([P, PH, TOPK, TOPK]), ALU.add))
                synced()
                base = made[0]
                top16([cand[:, h, :] for h in range(PH)], [cand2[:, h, :] for h in range(PH)],
                      [bs[:, h, :] for h in range(PH)], [bj[:, h, :] for h in range(PH)], PH,
                      lambda n: dve.wait_ge(cd, b * CD_N + (base + n)), cd)
                made[0] += 5 * PH + 4
                synced()
                step(nc.vector.tensor_scalar(bja[:, :, :], bj[:, :, :], 4, None, ALU.logical_shift_right))
                step(nc.vector.tensor_scalar(bjc[:, :, :], bj[:, :, :], 15, None, ALU.bitwise_and))
                step(nc.vector.tensor_tensor(bf[4][:, :, :], bs[:, :, :], bc(bs[:, :, 0], TOPK), ALU.subtract))
                assert made[0] == CD_EXP
                synced()
                step(nc.vector.tensor_copy(bf[0][:, :, :], bja[:, :, :]))
                step(nc.vector.tensor_copy(bf[1][:, :, :], bjc[:, :, :]))
                synced()
                for s_ in range(2):
                    io = iota[:, 0:TOPK].unsqueeze(1).to_broadcast([P, PH * TOPK, TOPK])
                    step(nc.vector.tensor_tensor(hot[s_][:, :, :, :].rearrange("p h k a -> p (h k) a"),
                                                 bc(bf[s_][:, :, :].rearrange("p h k -> p (h k)"), TOPK), io, ALU.is_equal))
                for s_ in range(2):
                    synced()
                    step(nc.vector.tensor_tensor(pick[:, :, :, :], hot[s_][:, :, :, :],
                                                 side(topi, s_).unsqueeze(2).to_broadcast([P, PH, TOPK, TOPK]), ALU.mult))
                    synced()
                    nc.vector.tensor_reduce(eidx[:, s_, :].rearrange("p (h k) -> p h k", h=PH), pick[:, :, :, :],
                                            AX.X, ALU.add).then_inc(cd_out, 1)
                    dve.wait_ge(cd_out, b * 3 + (s_ + 1))
                dve.wait_ge(cd_exp, b + 1)
                step(nc.vector.tensor_reduce(bf[6][:, :, 0], bf[5][:, :, :], AX.X, ALU.add))
                synced()
                step(nc.vector.reciprocal(bf[7][:, :, 0], bf[6][:, :, 0]))
                synced()
                nc.vector.tensor_tensor(eidx[:, 2, :].rearrange("p (h k) -> p h k", h=PH), bf[5][:, :, :],
                                        bc(bf[7][:, :, 0], TOPK), ALU.mult).then_inc(cd_out, 1)
                assert made[0] == CD_N

            dve.wait_ge(e_ev, LAT)
            with dve.Fori(0, SEQ // 8) as t:
                for z in range(2):
                    dve.wait_ge(g_mm, t * 2)
                    for w in range(4):
                        col = bass.ds(t * 8 + (4 * z + w), 1)
                        first_ = oh[:, z, w, 0, :]
                        nc.vector.tensor_scalar(first_, iota, eidT[:, 0, col], None, ALU.is_equal).then_inc(oh_done, 1)
                        nc.vector.tensor_scalar(oh[:, z, w, 1, :], iota, eidT[:, 1, col], eidT[:, 2, col],
                                                ALU.is_equal, ALU.mult).then_inc(oh_done, 1)

            def coefficients(i, x):
                slot = x // 4
                if x % 4 == 0:
                    dve.wait_ge(gq_full[slot], i * 16 + 16)
                    dve.wait_ge(gl_full[slot], i * 16 + 16)
                nc.vector.tensor_tensor(cf[:, x % 2, :].rearrange("p (g t) -> p g t", t=GTOK),
                                        gl[:, slot, x % 4, :].rearrange("p (g t) -> p g t", t=GTOK),
                                        gq[:, slot, :, x % 4, :], ALU.mult).then_inc(cf_done, 1)

            def low_parts(i, x):
                dve.wait_ge(ch, i * 8 + (x + 1))
                nc.vector.tensor_sub(c_lo[:, x % 4, :], cf[:, x % 2, :],
                                     c_hi[:, x % 4, :].bitcast(F32)).then_inc(cl, 1)
                dve.wait_ge(cl, i * 8 + (x + 1))

            for x in range(2):
                coefficients(0, x)
            with dve.Fori(0, N_IT) as i:
                for x in range(8):
                    low_parts(i, x)
                    coefficients(i + (x + 2) // 8, (x + 2) % 8)
            for x in range(8):
                low_parts(N_IT, x)
                if x < 6:
                    coefficients(N_IT, x + 2)
            for t in range(LAT):
                dve.wait_ge(fin_tr, t + 1)
                for i in range(2):
                    c = slice(i * 512, (i + 1) * 512)
                    nc.vector.scalar_tensor_tensor(xo[:, t, c], x1[:, t, c], ALPHA, bank[2 * (t % 2) + i][:, :],
                                                   ALU.mult, ALU.add).then_inc(xo_sum, 1)
            dve.wait_ge(ld_gb, 64)
            norm(xo, xo, 3, xo_sum, lambda t: 2 * t + 2, gb2)

        @block.tensor
        def _(pe):
            mm, transpose = nc.tensor.matmul, nc.tensor.transpose

            def ada_tile(tile, out):
                for k in range(KB):
                    last = mm(out, tile[:, k * P:(k + 1) * P], cond_s[:, k, :], start=k == 0, stop=k == KB - 1)
                last.then_inc(ada_mm, 1)

            pe.wait_ge(cond_done, 1)
            for m in range(ADA_FIRST):
                if m % 4 == 0:
                    pe.wait_ge(ada_in[m // 4], 64)
                ada_tile(first_ada(m), bank[7][:, 2 * m:2 * m + 2])
            pe.wait_ge(ld_cst, 16)
            pe.wait_ge(ln_out, NCH)
            for k in range(KB):
                if k >= 2:
                    pe.wait_ge(hin_mod, 2 * (k - 1))
                for t in range(NCH):
                    dst = bank[2 + k % 2][:, t * P:(t + 1) * P] if t < CT else bank[k % 2][:, (t - CT) * P:(t - CT + 1) * P]
                    last = transpose(dst, xin[:, t, k * P:(k + 1) * P], ident)
                last.then_inc(hin_tr, 1)
            pe.wait_ge(ab_split, 2)
            pe.wait_ge(hin_lo, 2 * KB)
            for xh, xl, out in ((lat_hi, lat_lo, bank[4][0:32, :]), (ctx_hi, ctx_lo, bank[5][0:32, 0:CTX])):
                for k in range(KB):
                    last = mm3(out, ab_hi[:, k, :], ab_lo[:, k, :], xh[:, k, :], xl[:, k, :], k == 0, k == KB - 1)
                last.then_inc(ab_mm, 1)
            def project(h, o, blocks):
                j = (0, 0, 1, 1, 2, 3)[o]
                xh, xl, n = (ctx_hi, ctx_lo, CTX) if o in (1, 3) else (lat_hi, lat_lo, SEQ)
                for k in blocks:
                    if k == 0:
                        pe.wait_ge(split_done, h * 4 + (j + 1))
                        if o == 0:
                            pe.wait_ge(mods_done, h + 2)
                        elif o == 2:
                            pe.wait_ge(z_done, h)
                        else:
                            pe.wait_ge(conv, h * 5 + max(o - 2, 0))
                    last = mm3(bank[P_BANK[o]][:, 0:n], *w_block(j, k), xh[:, k, :], xl[:, k, :], k == 0, k == KB - 1)
                    if k == KB - 1:
                        last.then_inc(proj, 1)

            def by_token(src, n, banks):
                for c in range(n):
                    last = transpose(bank[banks[c // 4]][:, (c % 4) * P:(c % 4 + 1) * P], src[:, c * P:(c + 1) * P], ident)
                last.then_inc(tr, 1)

            def squares(h):
                pe.wait_ge(sq_done, h * 2 + 2)
                for c in range(NCH + LAT):
                    last = mm(bank[3][:, LAT + c:LAT + c + 1], sqv[:, c * P:(c + 1) * P], ones[:, 0:1],
                              start=True, stop=True)
                last.then_inc(ssq, 1)

            def start_head(h):
                pe.wait_ge(gst_done, h + 1)
                pe.wait_ge(conv, h * 5 + 5)
                for g in range(NG):
                    for q in range(4):
                        last = mm(bank[5 + g][:, q * P:(q + 1) * P], gst[:, 4 * g + q, :], u_dir(q // 2), start=True, stop=True)
                    last.then_inc(gbc, 1)
                pe.wait_ge(silu, h * 5 + 5)
                pe.wait_ge(z_done, h + 1)
                by_token(kT, NCH, (0, 1))

            def pe_head(h, more):
                def ada_next(j):
                    pe.wait_ge(ada_full[j % 2], h * 32 + (j // 2 + 1) * 16)
                    ada_tile(ada[:, j % 2, :], bank[0][:, 2 * j:2 * j + 2])

                def by_channel(src, n, b0, count):
                    pe.wait_ge(kn, h * 3 + count)
                    for c in range(n):
                        last = transpose(bank[b0 + c // 4][:, (c % 4) * P:(c % 4 + 1) * P], src[:, c, :], ident)
                    last.then_inc(trb, 1)

                pe.wait_ge(dn_done, h)
                by_token(qT, LAT, (4,))
                by_channel(Kn, NCH, 2, 2)
                ada_next(0)
                by_channel(Qn, LAT, 4, 3)
                ada_next(1)
                pe.wait_ge(dm, h * 12 + 12)
                by_token(vT, NCH, (5, 6))
                ada_next(2)
                pe.wait_ge(knt, h * 3 + 3)
                for c in range(NCH):
                    kc = knT[:, c * P:(c + 1) * P]
                    last = mm(bank[2 + c // 4][:, (c % 4) * P:(c % 4 + 1) * P], kc, kc, start=True, stop=True)
                last.then_inc(kk, 1)
                for c in range(LAT):
                    last = mm(bank[4][:, c * P:(c + 1) * P], knT[:, (c + CT) * P:(c + CT + 1) * P],
                              qnT[:, c * P:(c + 1) * P], start=True, stop=True)
                last.then_inc(kk, 1)
                ada_next(3)
                pe.wait_ge(lt, h * 12 + 12)
                pe.wait_ge(att_done, h * 2 + 2)
                for g in range(NG):
                    for q in range(4):
                        last = transpose(bank[2 + g][:, q * P:(q + 1) * P], Lt[:, 4 * g + q, :], ident)
                    last.then_inc(n1, 1)
                pe.wait_ge(vev, h * 2 + 2)
                for g in range(NG):
                    pe.wait_ge(nn, h * 21 + (g + 1))
                    for q in range(4):
                        last = transpose(bank[5 + g][:, q * P:(q + 1) * P], eN[:, 4 * g + q, :], ident)
                    last.then_inc(xy, 1)

                def level(done, last_level):
                    for g in range(NG):
                        pe.wait_ge(y_done, done[1] + (g + 1))
                        for q in range(4):
                            last = mm(bank[2 + g][:, q * P:(q + 1) * P], Lt[:, 4 * g + q, :], dY[:, 4 * g + q, :],
                                      start=True, stop=True)
                        last.then_inc(n1, 1)
                    for g in range(NG):
                        pe.wait_ge(x_done, done[0] + (g - 2))
                        pe.wait_ge(nn, done[0] + (g + 1))
                        for q in range(4):
                            u, c = 4 * g + q, slice(q * P, (q + 1) * P)
                            if not last_level:
                                mm(bank[2 + g][:, c], gX[:, u, :], eN[:, u, :], start=True, stop=True)
                            last = mm(bank[5 + g][:, c], eN[:, u, :], gX[:, u, :], start=True, stop=True)
                        last.then_inc(xy, 1)

                with pe.Fori(1, LEVELS - 1) as lv:
                    level((h * 21 + lv * 3, h * 18 + lv * 3 - 3), False)
                level((h * 21 + (LEVELS - 1) * 3, h * 18 + (LEVELS - 2) * 3), True)
                pe.wait_ge(x_done, h * 21 + 21)
                pe.wait_ge(kts, h * 4 + 4)
                pe.wait_ge(kd_done, h * 2 + 2)
                first = True
                for s in range(NCH):
                    lat = s >= CT
                    for d in range(NDIR):
                        if not s:
                            continue
                        c = walk(d)[s]
                        pe.wait_ge(state, h * 10 + (2 * (s - 1) + d + 1))
                        mm(bank[3 + d][:, 0:P], kTs[:, unit(d, c), :], St[:, d, (s - 1) % 2, :], start=True,
                           stop=True).then_inc(ks, 1)
                        if lat:
                            mm(bank[2][:, (c - CT) * P:(c - CT + 1) * P], St[:, d, (s - 1) % 2, :],
                               qTs[:, (c - CT) // 2, d, (c % 2) * P:(c % 2 + 1) * P], start=first, stop=False,
                               skip_group_check=True)
                            first = False
                    if more:
                        project(h + 1, s, range(0, 3))
                    for d in range(NDIR):
                        c = walk(d)[s]
                        if s:
                            pe.wait_ge(res, h * 10 + (2 * (s - 1) + d + 1))
                        rhs = Rd[:, d, :] if s else Vt[:, c, :]
                        mm(bank[5 + d][:, 0:P], gX[:, unit(d, c), :], rhs, start=True, stop=True).then_inc(solve, 1)
                    if more:
                        project(h + 1, s, range(3, 5))
                    for d in range(NDIR):
                        c = walk(d)[s]
                        pe.wait_ge(vn, h * 12 + (2 * s + d + 1))
                        if s < NCH - 1:
                            mm(bank[3 + d][:, 0:P], Kd[:, unit(d, c), :], Vn[:, d, :], start=True,
                               stop=True).then_inc(kdv, 1)
                        if lat:
                            end = s == NCH - 1 and d == 1
                            last = mm(bank[2][:, (c - CT) * P:(c - CT + 1) * P], Vn[:, d, :],
                                      att[:, (c - CT) // 2, d, (c % 2) * P:(c % 2 + 1) * P], start=False, stop=end,
                                      skip_group_check=True)
                            if end:
                                last.then_inc(o_done, 1)
                    if more:
                        project(h + 1, s, range(5, KB))
                pe.wait_ge(sqo, h + 1)
                for c in range(LAT):
                    last = mm(bank[3][:, c:c + 1], cv[:, 1, c * P:(c + 1) * P], ones[:, 0:1], start=True, stop=True)
                last.then_inc(ssqo, 1)
                if more:
                    squares(h + 1)
                    start_head(h + 1)
                pe.wait_ge(rst_done, h + 1)
                for c in range(LAT):
                    last = mm(bank[4][:, c * P:(c + 1) * P], rst[:, c, :], ident, start=True, stop=True)
                last.then_inc(rbc_mm, 1)

            project(0, 0, range(KB))
            pe.wait_ge(ab_split, 4)
            for t in range(NCH):
                last = transpose(bank[6][:, t * 32:(t + 1) * 32], abT[0:32, t * P:(t + 1) * P], ident[0:32, 0:32])
            last.then_inc(ab_mm, 1)
            project(0, 1, range(KB))
            project(0, 2, range(0, 6))
            pe.wait_ge(gate_done, 2)
            for d in range(NDIR):
                v = gall[:, :].rearrange("p (a d c) -> p d a c", d=NDIR, c=2)[:, d]
                o = bank[5][:, 0:H * NU].rearrange("p (a d c) -> p d a c", d=NDIR, c=2)[:, d]
                mm(o, u_dir(d), v, start=True, stop=True).then_inc(cum_mm, 1)
            mm(bank[5][:, H * NU:2 * H * NU], ones, gall[:, :], start=True, stop=True).then_inc(cum_mm, 1)
            pe.wait_ge(gate_done, 5)
            project(0, 2, range(6, KB))
            for o in range(3, 6):
                project(0, o, range(KB))
            squares(0)
            start_head(0)
            with pe.Fori(0, H - 1) as h:
                pe_head(h, True)
            pe_head(H - 1, False)
            for m in range(FG):
                pe.wait_ge(split_done, T_F + m + 1)
                if m == 0:
                    pe.wait_ge(dn_done, H)
                if m >= 2:
                    pe.wait_ge(f_ev, m - 1)
                for k in range(KB):
                    last = mm3(bank[m % 2][:, :], *w_block(m, k), lat_hi[:, k, :], lat_lo[:, k, :], k == 0, k == KB - 1)
                last.then_inc(f_mm, 1)
            dft_c = cst[:, C_DFT:C_DFT + 2 * P]
            for e in range(2 * FG):
                pe.wait_ge(f_ev, e // 2 + 1)
                if e >= 4:
                    pe.wait_ge(fab_ev, e - 3)
                for b in range(2):
                    t = 2 * (e % 2) + b
                    last = mm(bank[2 + e % 4][:, b * 256:(b + 1) * 256], fT[:, e // 2, t * P:(t + 1) * P], dft_c,
                              start=True, stop=True)
                last.then_inc(fab_mm, 1)
            pe.wait_ge(ld_dft, 16)
            for m in range(FG):
                pe.wait_ge(fab_ev, 2 * m + 2)
                if m >= 2:
                    pe.wait_ge(fy_l, m - 1)
                for e in range(2):
                    for t in range(LAT):
                        last = mm(bank[6 + m % 2][:, :], fab[:, m, t, e * P:(e + 1) * P], dft[:, e, t, :],
                                  start=e + t == 0, stop=e == 1 and t == LAT - 1)
                last.then_inc(fy_mm, 1)
            pe.wait_ge(fy_l, FG)
            for m in range(KB):
                if m % 2 == 0:
                    pe.wait_ge(split_done, T_FOUR + m // 2 + 1)
                if m >= 2:
                    pe.wait_ge(four_ev, m - 1)
                for k in range(FG):
                    last = mm3(bank[m % 2][:, :], *w_block(m // 2, (m % 2) * FG + k), fy_hi[:, k, :], fy_lo[:, k, :],
                               k == 0, k == FG - 1)
                last.then_inc(four_mm, 1)
            pe.wait_ge(dnl, H)
            pe.wait_ge(four_ev, KB)
            with pe.Fori(0, 2) as i:
                for m in range(4):
                    for t in range(3):
                        n = 3 * m + t
                        pe.wait_ge(split_done, i * 12 + (T_MERGE + n + 1))
                        if m >= 2:
                            pe.wait_ge(mer_v, i * 12 + 3 * (m - 1))
                        xh, xl = (lat_hi, lat_lo) if t < 2 else (dn_hi, dn_lo)
                        for k in range(KB):
                            last = mm3(bank[3 * (m % 2) + t][:, :], *w_block(n % RING, k), xh[:, k, :], xl[:, k, :],
                                       k == 0, k == KB - 1)
                        last.then_inc(mer_mm, 1)
                pe.wait_ge(mer_v, i * 12 + 12)
            pe.wait_ge(mgl, KB)
            for m in range(KB):
                pe.wait_ge(split_done, T_OUT + m + 1)
                if m >= 2:
                    pe.wait_ge(yt_done, m - 1)
                for k in range(KB):
                    last = mm3(bank[m % 2][:, :], *w_block(m % RING, k), mg_hi[:, k, :], mg_lo[:, k, :],
                               k == 0, k == KB - 1)
                last.then_inc(out_mm, 1)
            pe.wait_ge(yt_done, KB)
            for t in range(LAT):
                if t >= 2:
                    pe.wait_ge(x1_sum, 2 * (t - 1))
                for k in range(KB):
                    last = transpose(bank[2 + 2 * (t % 2) + k // 4][:, (k % 4) * P:(k % 4 + 1) * P],
                                     yT[:, k, t * P:(t + 1) * P], ident)
                last.then_inc(ytr, 1)
            pe.wait_ge(ln_out, NCH + 2 * LAT)
            for k in range(KB):
                if k >= 2:
                    pe.wait_ge(h2_mod, k - 1)
                for t in range(LAT):
                    last = transpose(bank[k % 2][:, t * P:(t + 1) * P], xn[:, t, k * P:(k + 1) * P], ident)
                last.then_inc(h2_tr, 1)
            def pe_u(i, x):
                n = T_U - 2 * PH + x
                pe.wait_ge(split_done, i + (n + 1))
                pe.wait_ge(gelu, i + (x - 1))
                for k in range(KB):
                    last = mm3(bank[6 + x % 2][:, :], *w_block(n % RING, k), lat_hi[:, k, :], lat_lo[:, k, :],
                               k == 0, k == KB - 1)
                last.then_inc(a_mm, 1)

            pe.wait_ge(h2_lo, KB)
            pe.wait_ge(ld_sk, 16)
            with pe.Fori(0, 2 * PH // 4) as i:
                for j in range(4):
                    pe.wait_ge(split_done, i * 8 + (T_QUERY + 2 * j + 1))
                    pe.wait_ge(q_ev, i * 4 + max(j - 1, 0))
                    for k in range(KB):
                        last = mm3(bank[j % 2][:, :], *w_block(2 * j % RING, k), lat_hi[:, k, :], lat_lo[:, k, :],
                                   k == 0, k == KB - 1)
                    last.then_inc(q_mm, 1)
                    pe.wait_ge(split_done, i * 8 + (T_QUERY + 2 * j + 2))
                    pe.wait_ge(gelu, i * 4 + max(j - 1, 0))
                    for k in range(KB):
                        last = mm3(bank[6 + j % 2][:, :], *w_block((2 * j + 1) % RING, k), lat_hi[:, k, :], lat_lo[:, k, :],
                                   k == 0, k == KB - 1)
                    last.then_inc(a_mm, 1)
                    pe.wait_ge(q_ev, i * 4 + (j + 1))
                    pe.wait_ge(s_ev, i * 4 + max(j - 1, 0))
                    for b in range(LAT):
                        last = mm(bank[2 + j % 2][:, b * P:(b + 1) * P], qq[:, j, b * P:(b + 1) * P],
                                  sk[:, bass.ds(i * 4 + j, 1), :].rearrange("p o n -> p (o n)"), start=True, stop=True)
                    last.then_inc(s_mm, 1)
            with pe.Fori(0, LAT) as b:
                for j in range(U_CD):
                    pe_u(b * U_CD, X_CD + j)
                pe.wait_ge(cd_out, b * 3 + 3)
                pe.wait_ge(e_ev, b)
                for r_ in range(3):
                    last = transpose(bank[4][:, r_ * P:(r_ + 1) * P], eidx[:, r_, :], ident)
                last.then_inc(e_tr, 1)
            with pe.Fori(0, SEQ // 32) as i:
                for w in range(4):
                    for z in range(2):
                        pe.wait_ge(oh_done, i * 64 + (16 * w + 8 * z + 8))
                        if z == 0:
                            pe.wait_ge(g_ev, i * 8 + 2 * w)
                        for v in range(4):
                            last = mm(bank[z][:, v * P:(v + 1) * P], oh[:, z, v, 1, :], oh[:, z, v, 0, :],
                                      start=True, stop=True)
                        last.then_inc(g_mm, 1)
                    pe_u(i * 4, X_G + w)
            for x in range(X_END, PK):
                pe_u(0, x)

            def pe_v(i, y, start, stop):
                pe.wait_ge(split_done, i + (T_V + y + 1))
                pe.wait_ge(cl, i + (y + 1))
                for k in range(KB):
                    last = mm3(bank[k][:, :], *w_block(y % RING, k), c_hi[:, y % 4, :], c_lo[:, y % 4, :], start, stop)
                last.then_inc(v_mm, 1)

            pe.wait_ge(g_ev, SEQ // 4)
            pe.wait_ge(gelu, PK)
            for y in range(4):
                pe_v(0, y, y == 0, False)
            with pe.Fori(1, PK // 4 - 1) as i:
                for y in range(4):
                    pe_v(i * 4, y, False, False)
            for y in range(4):
                pe_v(0, PK - 4 + y, False, y == 3)
            pe.wait_ge(fin, KB)
            for t in range(LAT):
                if t >= 2:
                    pe.wait_ge(xo_sum, 2 * (t - 1))
                for k in range(KB):
                    last = transpose(bank[2 * (t % 2) + k // 4][:, (k % 4) * P:(k % 4 + 1) * P],
                                     acc[:, k, t * P:(t + 1) * P], ident)
                last.then_inc(fin_tr, 1)


def lay_out(x, c, ctx, c_ctx, w_ada, b_ada, w_in, conv_w, a_log, dt_bias, dn_norm_w, w_four, w_dn,
            w_out, ln_g, ln_b, peer_w_query, peer_sub_keys, peer_u, peer_v):
    f = np.float32

    def tiles(w):
        k, n = w.shape
        return w.reshape(k // P, P, n // P, P).transpose(2, 1, 0, 3)

    def flat(t):
        return np.ascontiguousarray(t, dtype=f).reshape(-1, P, KB * P)

    w_in = np.asarray(w_in[0])
    n_ab = 2 * NDIR * H
    wide = tiles(w_in[:, n_ab:])
    k_, v_, q_, z_ = (wide[i * H:(i + 1) * H] for i in range(4))
    f_ = wide[4 * H:4 * H + FG]
    g_ = wide[4 * H + FG:]
    four = tiles(np.asarray(w_four[0])).reshape(FG, 2, P, FG, P).transpose(0, 2, 1, 3, 4)
    dn_t = tiles(np.asarray(w_dn[0]))
    u = np.asarray(peer_u[0]).reshape(PK, PK, KB, P).transpose(0, 3, 2, 1).reshape(PK, P, KB * P)
    v = np.asarray(peer_v[0]).reshape(PK, P, KB * P)
    query = flat(tiles(np.asarray(peer_w_query[0])))
    order = [flat(np.stack([k_, v_, q_, z_], 1)), flat(f_), flat(four),
             flat(np.stack([g_[:KB], g_[KB:], dn_t], 1)), flat(tiles(np.asarray(w_out[0]))),
             flat(np.stack([query, u[:2 * PH]], 1)), flat(u[2 * PH:]), flat(v)]
    cst, dft = constants()
    two = np.stack([np.asarray(c)[0], np.asarray(c_ctx)], -1)
    return {
        "w": np.concatenate(order),
        "w_ada": flat(tiles(np.asarray(w_ada[0]))),
        "b_ada": np.ascontiguousarray(np.asarray(b_ada[0]).reshape(ADA_ALL, P).T),
        "cond": np.ascontiguousarray(two.reshape(KB, P, 2).transpose(1, 0, 2)),
        "x": np.ascontiguousarray(x[0]),
        "ctx": np.ascontiguousarray(ctx[0]),
        "cst": cst,
        "dft": dft,
        "ab_w": np.ascontiguousarray(w_in[:, :n_ab].reshape(KB, P, n_ab).transpose(1, 0, 2)),
        "dtb": np.ascontiguousarray(np.asarray(dt_bias[0]).reshape(-1)),
        "alog": np.ascontiguousarray(np.asarray(a_log[0]).reshape(-1)),
        "cw": np.ascontiguousarray(np.asarray(conv_w[0]).reshape(TAPS, 3 * H, P).transpose(2, 0, 1)),
        "nrm_w": np.ascontiguousarray(np.asarray(dn_norm_w[0]).reshape(P, 1)),
        "ln": np.ascontiguousarray(np.concatenate([np.asarray(ln_g[0]), np.asarray(ln_b[0])]).reshape(4, D)),
        "sub_keys": np.ascontiguousarray(np.asarray(peer_sub_keys[0]).reshape(2 * PH, PK, P).transpose(2, 0, 1)),
    }


def kernel(**inputs):
    import numpy as _np
    import concourse.bacc as _bacc
    from concourse.bass_utils import run_bass_kernel_spmd as _run

    nc = _bacc.Bacc("TRN2", target_bir_lowering=False, num_devices=1)
    arrays = lay_out(**inputs)
    aps = {n: nc.dram_tensor(n, a.shape, mybir.dt.from_np(a.dtype), kind="ExternalInput").ap() for n, a in arrays.items()}
    aps["out"] = nc.dram_tensor("out", (SEQ, D), F32, kind="ExternalOutput").ap()
    layer_kernel(nc, aps)
    r = _run(nc, [arrays], core_ids=[0])
    return _np.asarray(r.results[0]["out"]).reshape(1, SEQ, D)
```
